# Optimizing a Trainium2 kernel written in Bass

```python
import jax, jax.numpy as jnp
from jax import lax
import numpy as np

D_MODEL = 1024
BATCH = 1
SEQ = 1024
DEPTH = 2
DEC_BATCH = 8
DEC_SEQ = 1
PAST_LEN = 2048
PAGE_SIZE = 128

HEAD_DIM = 64
MIX_WIDTH = D_MODEL
N_HEADS = MIX_WIDTH // HEAD_DIM
H_A = N_HEADS // 2
H_B = N_HEADS - H_A
W_A = H_A * HEAD_DIM
W_B = H_B * HEAD_DIM
DILATED_PATTERNS = ((128, 1), (512, 4), (2048, 16))
WIN_MAX = max(w for w, _ in DILATED_PATTERNS)
BAND_BLOCK = 128
ROPE_THETA = 500000.0
ROT_DIM = HEAD_DIM // 4
MLSTM_CHUNK = 128
D_FF = 11 * D_MODEL // 4
CONV_W = 3
PLE_DIM = 256
RMS_EPS = 1e-6
NEG_INF = -1e30
IN_SPLITS = (W_A, 2 * W_A, 3 * W_A, 3 * W_A + W_B, 3 * W_A + 2 * W_B, 3 * W_A + 3 * W_B, 3 * W_A + 4 * W_B)
IN_COLS = 3 * W_A + 4 * W_B + 2 * H_B

kernel_name = 'dilated_mlstm_hybrid_step'

def rmsnorm(x, g):
    xf = x.astype(jnp.float32)
    y = xf * lax.rsqrt(jnp.mean(xf * xf, axis=-1, keepdims=True) + RMS_EPS)
    return (y * g.astype(jnp.float32)).astype(x.dtype)

def partial_rope(x, pos):
    half = ROT_DIM // 2
    inv = ROPE_THETA ** (-jnp.arange(half, dtype=jnp.float32) / half)
    ang = pos.astype(jnp.float32)[:, None] * inv[None, :]
    cos = jnp.cos(ang)[None, :, None, :]
    sin = jnp.sin(ang)[None, :, None, :]
    x1 = x[..., :half].astype(jnp.float32)
    x2 = x[..., half:ROT_DIM].astype(jnp.float32)
    r1 = (x1 * cos - x2 * sin).astype(x.dtype)
    r2 = (x2 * cos + x1 * sin).astype(x.dtype)
    return jnp.concatenate([r1, r2, x[..., ROT_DIM:]], axis=-1)

def mixer_inputs(h, w_in, q_norm, k_norm, b_gates, pos):
    B, T, _ = h.shape
    z = h @ w_in
    qa, ka, va, qb, kb, vb, ob, gates = jnp.split(z, IN_SPLITS, axis=-1)
    qa = partial_rope(rmsnorm(qa.reshape(B, T, H_A, HEAD_DIM), q_norm), pos)
    ka = partial_rope(rmsnorm(ka.reshape(B, T, H_A, HEAD_DIM), k_norm), pos)
    va = va.reshape(B, T, H_A, HEAD_DIM)
    to_heads = lambda t: jnp.transpose(t.reshape(B, T, H_B, HEAD_DIM), (0, 2, 1, 3)).astype(jnp.float32)
    qb = to_heads(qb)
    kb = to_heads(kb) * (HEAD_DIM ** -0.5)
    vb = to_heads(vb)
    g = gates.astype(jnp.float32) + b_gates.astype(jnp.float32)
    ig = jnp.transpose(g[..., :H_B], (0, 2, 1))
    lf = jnp.transpose(jax.nn.log_sigmoid(g[..., H_B:]), (0, 2, 1))
    og = jax.nn.sigmoid(ob)
    return qa, ka, va, qb, kb, vb, ig, lf, og

def dilated_band_stats(q, k, v, window, dilation):
    B, S, H, Dh = q.shape
    span = BAND_BLOCK * dilation
    S_pad = -(-S // span) * span
    L = S_pad // dilation
    nb = L // BAND_BLOCK
    pad = ((0, 0), (0, S_pad - S), (0, 0), (0, 0))

    def to_blocks(t):
        t = jnp.pad(t, pad).reshape(B, L, dilation, H, Dh).transpose(0, 2, 1, 3, 4)
        return t.reshape(B, dilation, nb, BAND_BLOCK, H, Dh).astype(jnp.float32)

    def with_prev(t):
        prev = jnp.pad(t, ((0, 0), (0, 0), (1, 0), (0, 0), (0, 0), (0, 0)))[:, :, :-1]
        return jnp.concatenate([prev, t], axis=3)

    qb = to_blocks(q)
    kk = with_prev(to_blocks(k))
    vv = with_prev(to_blocks(v))
    s = jnp.einsum('brnqhd,brnkhd->brnhqk', qb, kk) * (Dh ** -0.5)
    qi = jnp.arange(BAND_BLOCK)[:, None] + BAND_BLOCK
    kj = jnp.arange(2 * BAND_BLOCK)[None, :]
    dist = qi - kj
    band = (dist >= 0) & (dist <= window // dilation)
    first = (jnp.arange(nb)[:, None, None] > 0) | (kj[None] >= BAND_BLOCK)
    mask = band[None] & first
    s = jnp.where(mask[None, None, :, None], s, NEG_INF)
    m = jnp.max(s, axis=-1)
    e = jnp.exp(s - m[..., None])
    l = jnp.sum(e, axis=-1)
    o = jnp.einsum('brnhqk,brnkhd->brnqhd', e, vv) / jnp.transpose(l, (0, 1, 2, 4, 3))[..., None]
    o = o.reshape(B, dilation, L, H, Dh).transpose(0, 2, 1, 3, 4).reshape(B, S_pad, H, Dh)[:, :S]

    def back(t):
        t = jnp.transpose(t, (0, 1, 2, 4, 3)).reshape(B, dilation, L, H)
        return jnp.transpose(t, (0, 2, 1, 3)).reshape(B, S_pad, H)[:, :S]

    return back(m), back(l), o

def dilated_gather_stats(q, k_all, v_all, window, dilation, buf_len):
    T = q.shape[1]
    J = window // dilation + 1
    idx = buf_len + jnp.arange(T)[:, None] - dilation * jnp.arange(J)[None, :]
    valid = idx >= 0
    idxc = jnp.maximum(idx, 0)
    kg = jnp.take(k_all, idxc, axis=1).astype(jnp.float32)
    vg = jnp.take(v_all, idxc, axis=1).astype(jnp.float32)
    s = jnp.einsum('bthd,btjhd->bthj', q.astype(jnp.float32), kg) * (HEAD_DIM ** -0.5)
    s = jnp.where(valid[None, :, None, :], s, NEG_INF)
    m = jnp.max(s, axis=-1)
    e = jnp.exp(s - m[..., None])
    l = jnp.sum(e, axis=-1)
    o = jnp.einsum('bthj,btjhd->bthd', e, vg) / l[..., None]
    return m, l, o

def combine_by_denominators(stats):
    ms = jnp.stack([s[0] for s in stats])
    ls = jnp.stack([s[1] for s in stats])
    os_ = jnp.stack([s[2] for s in stats])
    M = jnp.max(ms, axis=0)
    w = ls * jnp.exp(ms - M)
    return jnp.sum(w[..., None] * os_, axis=0) / jnp.sum(w, axis=0)[..., None]

def mlstm_chunk(carry, inp):
    C, n, m = carry
    q, k, v, ig, lf = inp
    L = q.shape[2]
    b = jnp.cumsum(lf, axis=-1)
    causal = jnp.tril(jnp.ones((L, L), dtype=bool))
    dlog = jnp.where(causal, b[..., :, None] - b[..., None, :] + ig[..., None, :], NEG_INF)
    inter = b + m[..., None]
    m_t = jnp.maximum(inter, jnp.max(dlog, axis=-1))
    dw = jnp.exp(dlog - m_t[..., None])
    iw = jnp.exp(inter - m_t)
    sc = jnp.einsum('bhtk,bhsk->bhts', q, k) * dw
    num = iw[..., None] * jnp.einsum('bhvk,bhtk->bhtv', C, q) + jnp.einsum('bhts,bhsv->bhtv', sc, v)
    den = iw * jnp.einsum('bhk,bhtk->bht', n, q) + jnp.sum(sc, axis=-1)
    h = num / jnp.maximum(jnp.abs(den), jnp.exp(-m_t))[..., None]
    m_new = m_t[..., -1]
    ws = jnp.exp(b[..., -1:] - b + ig - m_new[..., None])
    cw = jnp.exp(b[..., -1] + m - m_new)
    C_new = cw[..., None, None] * C + jnp.einsum('bhs,bhsv,bhsk->bhvk', ws, v, k)
    n_new = cw[..., None] * n + jnp.einsum('bhs,bhsk->bhk', ws, k)
    return (C_new, n_new, m_new), h

def mlstm_prompt(q, k, v, ig, lf):
    B, H, S, Dh = q.shape
    nc = S // MLSTM_CHUNK
    chunks = lambda t: jnp.moveaxis(t.reshape(B, H, nc, MLSTM_CHUNK, *t.shape[3:]), 2, 0)
    init = (jnp.zeros((B, H, Dh, Dh), jnp.float32), jnp.zeros((B, H, Dh), jnp.float32),
            jnp.zeros((B, H), jnp.float32))
    carry, h = lax.scan(mlstm_chunk, init, (chunks(q), chunks(k), chunks(v), chunks(ig), chunks(lf)))
    h = jnp.moveaxis(h, 0, 2).reshape(B, H, S, Dh)
    return h, carry

def merge_heads(x, o_a, h_b, og, g_a, g_b, w_o):
    B, T, _ = x.shape
    ya = rmsnorm(o_a.reshape(B, T, W_A), g_a)
    yb = og.astype(jnp.float32) * rmsnorm(jnp.transpose(h_b, (0, 2, 1, 3)).reshape(B, T, W_B), g_b)
    y = jnp.concatenate([ya, yb], axis=-1).astype(x.dtype)
    return x + y @ w_o

def conv_glu(x, conv_buf, g_norm, w_up, conv_w, conv_b, w_down):
    h = rmsnorm(x, g_norm)
    gate, val = jnp.split(h @ w_up, 2, axis=-1)
    gp = jnp.concatenate([conv_buf.astype(gate.dtype), gate], axis=1)
    T = gate.shape[1]
    gc = conv_b + sum(conv_w[j] * gp[:, j:j + T] for j in range(CONV_W))
    y = jax.nn.gelu(gc) * val
    return x + y @ w_down, gp[:, -(CONV_W - 1):]

def per_layer_embed(x, p, g_norm, w_gate, w_proj):
    gate = jax.nn.sigmoid(rmsnorm(x, g_norm) @ w_gate)
    return x + gate * (p.astype(x.dtype) @ w_proj)

def setup_inputs(seed: int = 0) -> dict:
    key = jax.random.key(seed)
    ks = jax.random.split(key, 28)
    f32 = jnp.float32
    nrm = lambda k, shape, scale: jax.random.normal(k, shape, f32) * scale
    gain = lambda k, shape: 1.0 + 0.05 * jax.random.normal(k, shape, f32)
    w_buf = min(WIN_MAX, PAST_LEN)
    b_gates = jnp.concatenate([nrm(ks[10], (DEPTH, H_B), 0.1),
                               3.0 + 2.0 * jax.random.uniform(ks[11], (DEPTH, H_B), f32)], axis=-1)
    return {
        'x_prompt': nrm(ks[0], (BATCH, SEQ, D_MODEL), 1.0),
        'x_sample': nrm(ks[1], (DEC_BATCH, DEC_SEQ, D_MODEL), 1.0),
        'cache_win_k': nrm(ks[2], (DEPTH, DEC_BATCH, w_buf, H_A, HEAD_DIM), 1.0),
        'cache_win_v': nrm(ks[3], (DEPTH, DEC_BATCH, w_buf, H_A, HEAD_DIM), 1.0),
        'state_C': nrm(ks[4], (DEPTH, DEC_BATCH, H_B, HEAD_DIM, HEAD_DIM), 0.1),
        'state_n': nrm(ks[5], (DEPTH, DEC_BATCH, H_B, HEAD_DIM), 0.5),
        'state_m': nrm(ks[6], (DEPTH, DEC_BATCH, H_B), 0.5),
        'state_conv': nrm(ks[7], (DEPTH, DEC_BATCH, CONV_W - 1, D_FF), 1.0),
        'p_prompt': nrm(ks[8], (DEPTH, BATCH, SEQ, PLE_DIM), 1.0),
        'p_sample': nrm(ks[9], (DEPTH, DEC_BATCH, DEC_SEQ, PLE_DIM), 1.0),
        'norm_mix': gain(ks[12], (DEPTH, D_MODEL)),
        'w_in': nrm(ks[13], (DEPTH, D_MODEL, IN_COLS), D_MODEL ** -0.5),
        'q_norm': gain(ks[14], (DEPTH, HEAD_DIM)),
        'k_norm': gain(ks[15], (DEPTH, HEAD_DIM)),
        'b_gates': b_gates,
        'out_norm_a': gain(ks[16], (DEPTH, W_A)),
        'out_norm_b': gain(ks[17], (DEPTH, W_B)),
        'w_out': nrm(ks[18], (DEPTH, MIX_WIDTH, D_MODEL), MIX_WIDTH ** -0.5),
        'norm_ffn': gain(ks[19], (DEPTH, D_MODEL)),
        'w_up': nrm(ks[20], (DEPTH, D_MODEL, 2 * D_FF), D_MODEL ** -0.5),
        'conv_w': nrm(ks[21], (DEPTH, CONV_W, D_FF), CONV_W ** -0.5),
        'conv_b': nrm(ks[22], (DEPTH, D_FF), 0.02),
        'w_down': nrm(ks[23], (DEPTH, D_FF, D_MODEL), D_FF ** -0.5),
        'norm_ple': gain(ks[24], (DEPTH, D_MODEL)),
        'w_ple_gate': nrm(ks[25], (DEPTH, D_MODEL, D_MODEL), D_MODEL ** -0.5),
        'w_ple_proj': nrm(ks[26], (DEPTH, PLE_DIM, D_MODEL), PLE_DIM ** -0.5),
    }

def reference(x_prompt, x_sample, cache_win_k, cache_win_v, state_C, state_n, state_m, state_conv,
              p_prompt, p_sample, norm_mix, w_in, q_norm, k_norm, b_gates, out_norm_a, out_norm_b,
              w_out, norm_ffn, w_up, conv_w, conv_b, w_down, norm_ple, w_ple_gate, w_ple_proj):
    seq = x_prompt.shape[1]
    dec_seq = x_sample.shape[1]
    buf_len = cache_win_k.shape[2]
    keep_p = min(WIN_MAX, seq)
    pos_p = jnp.arange(seq, dtype=jnp.int32)
    pos_s = PAST_LEN + jnp.arange(dec_seq, dtype=jnp.int32)
    xp, xs = x_prompt, x_sample
    wk_p, wv_p, C_p, n_p, m_p, cv_p = [], [], [], [], [], []
    wk_s, wv_s, C_s, n_s, m_s, cv_s = [], [], [], [], [], []
    for i in range(DEPTH):
        qa, ka, va, qb, kb, vb, ig, lf, og = mixer_inputs(rmsnorm(xp, norm_mix[i]), w_in[i], q_norm[i],
                                                          k_norm[i], b_gates[i], pos_p)
        o_a = combine_by_denominators([dilated_band_stats(qa, ka, va, w, d) for (w, d) in DILATED_PATTERNS])
        h_b, (c_new, n_new, m_new) = mlstm_prompt(qb, kb, vb, ig, lf)
        xp = merge_heads(xp, o_a, h_b, og, out_norm_a[i], out_norm_b[i], w_out[i])
        conv0 = jnp.zeros((xp.shape[0], CONV_W - 1, D_FF), xp.dtype)
        xp, conv_new = conv_glu(xp, conv0, norm_ffn[i], w_up[i], conv_w[i], conv_b[i], w_down[i])
        xp = per_layer_embed(xp, p_prompt[i], norm_ple[i], w_ple_gate[i], w_ple_proj[i])
        wk_p.append(ka[:, seq - keep_p:])
        wv_p.append(va[:, seq - keep_p:])
        C_p.append(c_new)
        n_p.append(n_new)
        m_p.append(m_new)
        cv_p.append(conv_new)
        qa, ka, va, qb, kb, vb, ig, lf, og = mixer_inputs(rmsnorm(xs, norm_mix[i]), w_in[i], q_norm[i],
                                                          k_norm[i], b_gates[i], pos_s)
        k_all = jnp.concatenate([cache_win_k[i].astype(ka.dtype), ka], axis=1)
        v_all = jnp.concatenate([cache_win_v[i].astype(va.dtype), va], axis=1)
        o_a = combine_by_denominators([dilated_gather_stats(qa, k_all, v_all, w, d, buf_len)
                                       for (w, d) in DILATED_PATTERNS])
        carry0 = (state_C[i].astype(jnp.float32), state_n[i].astype(jnp.float32), state_m[i].astype(jnp.float32))
        (c_new, n_new, m_new), h_b = mlstm_chunk(carry0, (qb, kb, vb, ig, lf))
        xs = merge_heads(xs, o_a, h_b, og, out_norm_a[i], out_norm_b[i], w_out[i])
        xs, conv_new = conv_glu(xs, state_conv[i], norm_ffn[i], w_up[i], conv_w[i], conv_b[i], w_down[i])
        xs = per_layer_embed(xs, p_sample[i], norm_ple[i], w_ple_gate[i], w_ple_proj[i])
        wk_s.append(ka)
        wv_s.append(va)
        C_s.append(c_new)
        n_s.append(n_new)
        m_s.append(m_new)
        cv_s.append(conv_new)
    st = jnp.stack
    return (xp, xs, st(wk_p), st(wv_p), st(C_p), st(n_p), st(m_p), st(cv_p),
            st(wk_s), st(wv_s), st(C_s), st(n_s), st(m_s), st(cv_s))


_drawn_inputs = setup_inputs


def setup_inputs(seed=0):
    import zlib

    import numpy as np

    out = dict(_drawn_inputs(seed))
    spreads = {}
    factors = {'conv_b': 3.434, 'norm_ple': 4.709}
    for name, (base, spread) in spreads.items():
        noise = np.random.default_rng([zlib.crc32(name.encode()), seed]).standard_normal(out[name].shape)
        drawn = base * np.exp(spread * noise) if base else spread * noise
        out[name] = __import__('jax').numpy.asarray(drawn.astype(out[name].dtype))
    for name, factor in factors.items():
        out[name] = (out[name] * factor).astype(out[name].dtype)
    return out
```

```python
from contextlib import ExitStack

import numpy as np

import concourse.bass as bass
from concourse import mybir

F32 = mybir.dt.float32
F32R = mybir.dt.float32r
ALU = mybir.AluOpType
ACT = mybir.ActivationFunctionType
AX = mybir.AxisListType

P = 128
D = 1024
KT = D // P
SEQ = 1024
DEPTH = 2
NB = 8
TOK = SEQ + NB
NT = SEQ // P
CH = TOK // 3
PAST = 2048
HD = 64
NH = 8
WA = NH * HD
PAIRS = NH // 2
RH = 8
DFF = 2816
FT = DFF // P
FG = FT // 2
CW = 3
PLE = 256
EPS = 1e-6
SCALE = HD ** -0.5
NEG = -1e30
WBLK = 2048
NSLOT = 3
ZW = 4 * P + 2
VO = 2 * P
OG = VO + 2 * (HD + 1)
DIL = ((128, 1), (512, 4), (2048, 16))


def rows(t):
    return P if t < NT else NB


def tok(t):
    return slice(t * P, t * P + rows(t))


def chunk_of(t):
    return (t * P + rows(t) - 1) // CH


def col(c):
    return slice(c * CH, (c + 1) * CH)


class Steps:

    def __init__(self, eng, step):
        self.eng, self.step, self.n, self.turn, self.per = eng, step, {}, None, {}

    def __call__(self, ins, sem=None, wait=True):
        sem = self.step if sem is None else sem
        key = sem.name
        self.n[key] = self.n.get(key, 0) + 1
        ins.then_inc(sem, 1)
        if wait:
            value = self.n[key]
            if self.turn is not None:
                value = self.turn * self.per[key] + value
            self.eng.wait_ge(sem, value)

    def loop(self, turn, per):
        self.turn, self.per = turn, {s.name: k for s, k in per.items()}
        self.start = dict(self.n)

    def end_loop(self, turns):
        for key, k in self.per.items():
            assert self.n.get(key, 0) - self.start.get(key, 0) == k, (key, self.n.get(key, 0) - self.start.get(key, 0), k)
            self.n[key] = self.start.get(key, 0) + k * turns
        for key in self.n:
            assert key in self.per or self.n[key] == self.start[key], key
        self.turn = None


def block_list():
    out = [("gates", 0, 1, KT * 2 * NH, 1)]
    for p in range(2 * PAIRS):
        n = 3 if p < PAIRS else 4
        for half in (0, 1):
            out.append(("in", 2 * p + half, n, 4 * n * P, GEMM_IN + (NT + 1) * (p + 1)))
    for b in range(4):
        out.append(("out", b, 1, WBLK, GEMM_OUT + 6 * (b + 1)))
    for i in range(FG):
        out.append(("gate", i, 1, WBLK, GEMM_FFN + 36 * i + 9))
        out.append(("val", i, 1, WBLK, GEMM_FFN + 36 * i + 12))
        out.append(("down", i, 1, WBLK, GEMM_FFN + 36 * i + 36))
    for b in range(4):
        out.append(("pg", b, 1, WBLK, GEMM_PLE + 12 * (b + 1)))
        out.append(("pp", b, 1, 2 * 256, GEMM_PLE + 12 * (b + 1)))
    return out


GEMM_IN = 1
GEMM_OUT = GEMM_IN + 2 * PAIRS * (NT + 1)
GEMM_FFN = GEMM_OUT + 24
GEMM_PLE = GEMM_FFN + 36 * FG
BLOCKS = block_list()
B_IN, B_OUT, B_FFN = 1, 1 + 4 * PAIRS, 1 + 4 * PAIRS + 4
B_PLE = B_FFN + 3 * FG


def raw_value(n):
    return 16 * sum(BLOCKS[m][2] for m in range(n % NSLOT, n + 1, NSLOT))


UNITS = [(e, qb) for e in (0, 1) for qb in range(NT)]


def far(u):
    return sum(1 for x in range(u) if x % NT >= 4)


def build(nc, A, O):
    with ExitStack() as ctx:
        def sb(name, shape, dt=F32, stack=ctx):
            return stack.enter_context(nc.sbuf_tensor(name, shape, dt))

        def sem(name):
            return ctx.enter_context(nc.semaphore(name))

        hi = sb("hi", [P, KT, TOK], F32R)
        lo = sb("lo", [P, KT, TOK], F32R)
        raw = sb("raw", [P, NSLOT, WBLK])
        whi = sb("whi", [P, NSLOT, WBLK], F32R)
        wlo = sb("wlo", [P, NSLOT, WBLK], F32R)
        ident = sb("ident", [P, P])
        ones = sb("ones", [P, P])
        rstd = sb("rstd", [P, TOK])
        rcol = sb("rcol", [P, NT + 1])
        gst = sb("gst", [3 * KT, P])
        gains = sb("gains", [P, 3 * KT])
        bgate = sb("bgate", [P, 2 * NH])
        qkg = sb("qkg", [P, 4, HD])
        cvec = sb("cvec", [P, FT, 2 * NB + CW + 1])
        tail = sb("tail", [P, FT, 2 + NB])
        gz = sb("gz", [P, NT + 1, 2 * NH])
        gt = sb("gt", [P, NT + 1, NH])
        ssq = sb("ssq", [P, 2 * (NT + 1)])
        yrs = sb("yrs", [P, 2 * (NT + 1)])
        yt2 = sb("yt2", [P, 2 * (NT + 1)])
        rope = sb("rope", [P, NT + 1, 4 * RH])
        cvt = sb("cvt", [P, 2 * NB + CW + 1])
        eps = sb("eps", [P, 1])
        one1 = sb("one1", [P, 1])
        mid = ctx.enter_context(ExitStack())
        zt = sb("zt", [P, NT + 1, ZW], F32, mid)
        qT = sb("qT", [P, SEQ], F32, mid)
        kT = sb("kT", [P, SEQ], F32, mid)
        yb = sb("yb", [P, NT, P], F32, mid)
        sel = sb("sel", [NH, NH, P], F32, mid)
        att = sb("att", [P, 4096], F32, mid)
        rowr = sb("rowr", [P, SEQ], F32, mid)
        rowi = sb("rowi", [NH, SEQ], F32, mid)
        mask = sb("mask", [P, SEQ], F32, mid)
        causal = sb("causal", [P, P], F32, mid)
        uc = sb("uc", [P, NT, NH], F32, mid)
        em = sb("em", [P, NT, NH], F32, mid)
        mprev = sb("mprev", [NH, NT], F32, mid)
        nm = sb("nm", [P, 2], F32, mid)
        den = sb("den", [P, 2], F32, mid)
        qs36 = sb("qs36", [P, 3, 4 * (NT + 1)], F32, mid)
        Cst = sb("Cst", [P, 2 * (HD + 1)], F32, mid)
        cwb = sb("cwb", [P, NT], F32, mid)
        cT = sb("cT", [HD, P], F32, mid)
        small = sb("small", [HD, 16], F32, mid)
        zb = sb("zb", [HD, 7, HD], F32, mid)
        sv = sb("sv", [HD, 4, HD], F32, mid)
        mid.close()
        late = ctx.enter_context(ExitStack())
        X = sb("X", [P, KT, TOK], F32, late)
        yhi = sb("yhi", [P, 2, TOK], F32R, late)
        ylo = sb("ylo", [P, 2, TOK], F32R, late)
        wa = sb("wa", [P, TOK + 4], F32, late)
        wb = sb("wb", [P, TOK], F32, late)
        sq = sb("sq", [P, 2, TOK], F32, late)
        ps = ctx.enter_context(nc.psum_tensor("ps", [P, 8, 512], F32))

        Xd = nc.dram_tensor("x_scratch", [P, KT, TOK], F32).ap()
        Yd = nc.dram_tensor("y_scratch", [TOK, D], F32).ap()
        Zd = nc.dram_tensor("z_scratch", [NB, 7, WA], F32).ap()
        Gd = nc.dram_tensor("g_scratch", [NB, 2, NH], F32).ap()
        Hd = nc.dram_tensor("h_scratch", [NB, WA], F32).ap()
        Ad = nc.dram_tensor("a_scratch", [NB, WA], F32).ap()

        const_in = sem("const_in")
        const_set = sem("const_set")
        x_in = [sem("x_in0"), sem("x_in1")]
        x_turned = sem("x_turned")
        x_evac_a, x_evac_v = sem("x_evac_a"), sem("x_evac_v")
        fin_turned, fin_evac_a, fin_evac_v = sem("fin_turned"), sem("fin_evac_a"), sem("fin_evac_v")
        y_stored = [sem("y_stored0"), sem("y_stored1")]
        act_step0, dve_step0 = sem("act_step0"), sem("dve_step0")
        engines_done, layer_open, settled = sem("engines_done"), sem("layer_open"), sem("settled")

        layer_sems = []

        def lsem(name):
            s = sem(name)
            layer_sems.append(s)
            return s

        act_step, dve_step, pool_step = lsem("act_step"), lsem("dve_step"), lsem("pool_step")
        raw_in = [lsem(f"raw_in{s}") for s in range(NSLOT)]
        w_split = lsem("w_split")
        gemm_done = lsem("gemm_done")
        vec_in, gst_in, cs_in, cs_t, gst_t, cvec_done, gains_done = [lsem(n) for n in (
            "vec_in", "gst_in", "cs_in", "cs_t", "gst_t", "cvec_done", "gains_done")]
        x_spilled, x_back, ygain_in = lsem("x_spilled"), lsem("x_back"), lsem("ygain_in")
        split_hi, split_lo, sq_ready, sq_used = [lsem(n) for n in ("split_hi", "split_lo", "sq_ready", "sq_used")]
        ss_ready, rs_first, rstd_done, rcol_ready, rcol_done = [lsem(n) for n in (
            "ss_ready", "rs_first", "rstd_done", "rcol_ready", "rcol_done")]
        gz_abs, gz_ln, lf_done, gates_read = [lsem(n) for n in ("gz_abs", "gz_ln", "lf_done", "gates_read")]
        z_done, qk_ssq, qk_rs, qk_norm, turned, q_evac, k_evac = [lsem(n) for n in (
            "z_done", "qk_ssq", "qk_rs", "qk_norm", "turned", "q_evac", "k_evac")]
        s_ready, s_masked, p_done, t0_ready, t1_ready, pt0, pt1, o_ready, o_read = [lsem(n) for n in (
            "s_ready", "s_masked", "p_done", "t0_ready", "t1_ready", "pt0", "pt1", "o_ready", "o_read")]
        o_exp = lsem("o_exp")
        yb_done, yb_stored, z_stored = lsem("yb_done"), lsem("yb_stored"), lsem("z_stored")
        gr_ready, rows_done, r2_done, iw_done, gc_ready, uc_done, em_done, mg_stored = [lsem(n) for n in (
            "gr_ready", "rows_done", "r2_done", "iw_done", "gc_ready", "uc_done", "em_done", "mg_stored")]
        ib_ready, rb_ready, ib_used, rm_done, d_done, og_done = [lsem(n) for n in (
            "ib_ready", "rb_ready", "ib_used", "rm_done", "d_done", "og_done")]
        a_ready, sc_done, ws_done, n_ready, n_read, u_ready, c_upd, ct_ready, ct_done, c_stored = [lsem(n) for n in (
            "a_ready", "sc_done", "ws_done", "n_ready", "n_read", "u_ready", "c_upd", "ct_ready", "ct_done", "c_stored")]
        zb_in, kq_in, kq_used, st_ready, sm_new, sp_max, sp_exp, pj_ready, pj_back, pj_done = [lsem(n) for n in (
            "zb_in", "kq_in", "kq_used", "st_ready", "sm_new", "sp_max", "sp_exp", "pj_ready", "pj_back", "pj_done")]
        kv_in = [lsem(f"kv_in{s}") for s in range(3)]
        q_in = [lsem(f"q_in{s}") for s in range(2)]
        v_used, ot_done, so_ready, so_done, as_stored, as_in, sc_exp_in, sc_exp, ys_done, ys_stored = [lsem(n) for n in (
            "v_used", "ot_done", "so_ready", "so_done", "as_stored", "as_in", "sc_exp_in", "sc_exp", "ys_done", "ys_stored")]
        cst_in, cst_out, s_scores = lsem("cst_in"), lsem("cst_out"), lsem("s_scores")
        ys_in, ssq_done, yrs_first, yt_ready, yn_done, yh_done, yl_done = [lsem(n) for n in (
            "ys_in", "ssq_done", "yrs_first", "yt_ready", "yn_done", "yh_done", "yl_done")]
        yst_in = [lsem("yst_in0"), lsem("yst_in1")]
        wo_done = lsem("wo_done")
        gate_read, conv_1, conv_done, gelu_done, y_val, y_hi, y_lo, dn_read = [lsem(n) for n in (
            "gate_read", "conv_1", "conv_done", "gelu_done", "y_val", "y_hi", "y_lo", "dn_read")]
        conv_a = lsem("conv_a")
        pst_in = [lsem("pst_in0"), lsem("pst_in1")]
        pt_ready, pt_hi, pt_lo, pg_sc, pg_exp, ple_done = [lsem(n) for n in (
            "pt_ready", "pt_hi", "pt_lo", "pg_sc", "pg_exp", "ple_done")]
        tl_ready, tl_done, tl_stored, cs_copied = lsem("tl_ready"), lsem("tl_done"), lsem("tl_stored"), lsem("cs_copied")

        ctx.enter_context(nc.allow_non_contiguous_dma(reason="small vectors"))
        block = ctx.enter_context(nc.Block())

        def layer(ap, l):
            names = "abcdef"[:len(ap.shape) - 1]
            return ap[bass.ds(l, 1)].rearrange(f"z a {' '.join(names[1:])} -> (z a) {' '.join(names[1:])}")

        def weight_sources(l, n, i=None):
            kind, j, _, used, _ = BLOCKS[n]
            s = n % NSLOT
            dst = raw[:, s, 0:used]
            w_in = layer(A["w_in"], l).rearrange("(k p) n -> p k n", p=P)
            if kind == "gates":
                return [(dst.rearrange("p (k n) -> p k n", k=KT), w_in[:, :, 3 * WA + 4 * WA:])]
            if kind == "in":
                p, half = j // 2, j % 2
                first, cnt = (0, 3) if p < PAIRS else (3, 4)
                dst = dst.rearrange("p (k c n) -> p k c n", k=4, n=P)
                at = [(first + c) * WA + (p % PAIRS) * P for c in range(cnt)]
                return [(dst[:, :, c, :], w_in[:, 4 * half:4 * half + 4, at[c]:at[c] + P]) for c in range(cnt)]
            if kind in ("out", "pg"):
                w = layer(A["w_out" if kind == "out" else "w_ple_gate"], l).rearrange("(k p) n -> p k n", p=P)
                return [(dst.rearrange("p (k n) -> p k n", k=KT), w[:, :, 256 * j:256 * j + 256])]
            if kind == "pp":
                w = layer(A["w_ple_proj"], l).rearrange("(k p) n -> p k n", p=P)
                return [(dst.rearrange("p (k n) -> p k n", k=2), w[:, :, 256 * j:256 * j + 256])]
            i = j if i is None else i
            if kind == "down":
                w = layer(A["w_down"], l)[bass.ds(i * 256, 256), :].rearrange("(k p) n -> p k n", p=P)
                return [(dst.rearrange("p (k n) -> p k n", k=2), w)]
            w = layer(A["w_up"], l).rearrange("(k p) n -> p k n", p=P)
            return [(dst.rearrange("p (k n) -> p k n", k=KT), w[:, :, bass.ds(i * 256 + (DFF if kind == "val" else 0), 256)])]

        @block.sync
        def _(sp):
            def load_block(l, n):
                if n >= NSLOT:
                    sp.wait_ge(w_split, n - NSLOT + 1)
                for dst, src in weight_sources(l, n):
                    sp.dma_start(dst, src).then_inc(raw_in[n % NSLOT], 16)

            n_const = 0
            for dst, src in ((ident[:, :], A["c_ident"]), (rope[:, :, :], A["c_rope"])):
                sp.dma_start(dst, src).then_inc(const_in, 16)
                n_const += 1
            for t in range(NT + 1):
                if t >= 2:
                    sp.wait_ge(x_turned, t - 1)
                src = A["x_prompt"][0, tok(t), :] if t < NT else A["x_sample"][:, 0, :]
                stage = (wa, wb)[t % 2]
                sp.dma_start(stage[0:rows(t), 0:D], src).then_inc(x_in[t % 2], 16)

            sp.wait_ge(x_evac_a, NT + 1)
            sp.wait_ge(x_evac_v, NT + 1)
            with sp.Fori(0, DEPTH) as l:
                for j, name in enumerate(("norm_mix", "norm_ffn", "norm_ple")):
                    sp.dma_start(gst[j * KT:(j + 1) * KT, :],
                                 A[name][bass.ds(l, 1), :].rearrange("z (k p) -> (z k) p", p=P)).then_inc(gst_in, 16)
                for n in range(3):
                    load_block(l, n)
                sp.dma_start(Xd, X[:, :, :]).then_inc(x_spilled, 16)
                stc = att[:, 0:DFF]
                sp.dma_start(stc[0:2 * NB, :], layer(A["state_conv"], l).rearrange("b j f -> (b j) f")).then_inc(cs_in, 16)
                sp.dma_start(stc[2 * NB:2 * NB + CW, :], layer(A["conv_w"], l)).then_inc(cs_in, 16)
                sp.dma_start(stc[2 * NB + CW:2 * NB + CW + 1, :], A["conv_b"][bass.ds(l, 1), :]).then_inc(cs_in, 16)
                sp.dma_start(bgate[:, :], A["b_gates"][bass.ds(l, 1), :].to_broadcast([P, 2 * NH])).then_inc(vec_in, 16)
                for j in range(4):
                    g = A["q_norm" if j < 2 else "k_norm"][bass.ds(l, 1), :]
                    sp.dma_start(qkg[:, j, :], g.to_broadcast([P, HD])).then_inc(vec_in, 16)
                sp.dma_start(layer(O["conv_s"], l)[:, 0, :], layer(A["state_conv"], l)[:, 1, :]).then_inc(cs_copied, 16)
                sp.wait_ge(x_spilled, 16)
                sp.wait_ge(sq_used, KT)
                sp.dma_start(sel[:, :, :], A["c_sel"]).then_inc(vec_in, 16)
                sp.wait_ge(rstd_done, 1)
                sp.dma_start(mask[:, :], A["c_mask"]).then_inc(vec_in, 16)
                sp.dma_start(causal[:, :], A["c_causal"]).then_inc(vec_in, 16)
                for n in range(3, 9):
                    load_block(l, n)
                for p in range(2 * PAIRS):
                    h2 = p % PAIRS
                    first = 0 if p < PAIRS else 3
                    if p == PAIRS:
                        sp.wait_ge(rows_done, 1)
                        sp.dma_start(Gd[:, 0, :], gz[0:NB, NT, 0:NH]).then_inc(mg_stored, 16)
                        sp.dma_start(Gd[:, 1, :], gz[0:NB, NT, NH:2 * NH]).then_inc(mg_stored, 16)
                        m_row = att[0:NH, 3 * SEQ + SEQ - 1:4 * SEQ]
                        sp.dma_start(layer(O["m_p"], l).rearrange("z h -> h z"), m_row).then_inc(mg_stored, 16)
                    if p < PAIRS:
                        sp.wait_ge(qk_norm, p + 1)
                    else:
                        sp.wait_ge(og_done, h2 + 1)
                    cols = slice(h2 * P, h2 * P + P)
                    parts = [zt[:, :, 0:P], zt[:, :, P:2 * P]]
                    for c in range(2):
                        sp.dma_start(Zd[:, first + c, cols], parts[c][0:NB, NT, :]).then_inc(z_stored, 16)
                    vv = zt[0:NB, NT, VO:OG].rearrange("p (e d) -> p e d", e=2)[:, :, 0:HD]
                    sp.dma_start(Zd[:, first + 2, cols].rearrange("b (e d) -> b e d", e=2), vv).then_inc(z_stored, 16)
                    if p < PAIRS:
                        ko = layer(O["wk_p"], l).rearrange("z (t p) h d -> p (z t) (h d)", p=P)
                        sp.dma_start(ko[:, :, cols], zt[:, 0:NT, P:2 * P]).then_inc(z_stored, 16)
                        vo = layer(O["wv_p"], l).rearrange("z (t p) h d -> p (z t) h d", p=P)
                        for e in range(2):
                            at = VO + e * (HD + 1)
                            sp.dma_start(vo[:, :, 2 * h2 + e, :], zt[:, 0:NT, at:at + HD]).then_inc(z_stored, 16)
                        ks = layer(O["wk_s"], l).rearrange("b z h d -> b (z h d)")
                        sp.dma_start(ks[:, cols], zt[0:NB, NT, P:2 * P]).then_inc(z_stored, 16)
                        vs = layer(O["wv_s"], l).rearrange("b z h d -> b (z h) d")
                        sp.dma_start(vs[:, 2 * h2:2 * h2 + 2, :], vv).then_inc(z_stored, 16)
                    else:
                        sp.dma_start(Zd[:, 6, cols], zt[0:NB, NT, OG:ZW]).then_inc(z_stored, 16)
                    sp.wait_ge(yb_done, p + 1)
                    yv = Yd[0:SEQ, p * P:p * P + P].rearrange("(t p) c -> p t c", p=P)
                    sp.dma_start(yv, yb[:, :, :]).then_inc(yb_stored, 16)
                    if p >= PAIRS:
                        sp.wait_ge(ct_done, h2 + 1)
                        cp = layer(O["C_p"], l).rearrange("z h v k -> v (z h) k")
                        sp.dma_start(cp[:, 2 * h2:2 * h2 + 2, :], cT[:, :].rearrange("v (h k) -> v h k", h=2)).then_inc(c_stored, 16)
                        npv = layer(O["n_p"], l).rearrange("z h k -> (z h k)").rearrange("(q a) -> q a", a=1)
                        for e in range(2):
                            at = e * (HD + 1) + HD
                            sp.dma_start(npv[h2 * P + e * HD:h2 * P + (e + 1) * HD, :], Cst[e * HD:(e + 1) * HD, at:at + 1]).then_inc(c_stored, 16)
                    for n in (9 + 2 * p, 10 + 2 * p):
                        if n < B_FFN + 2:
                            load_block(l, n)
                sp.wait_ge(z_stored, 16 * (PAIRS * 8 + PAIRS * 4))
                sp.wait_ge(mg_stored, 48)
                sp.wait_ge(yb_stored, 16 * 2 * PAIRS)
                for b in range(NB):
                    sp.dma_start(zb[b * NH:(b + 1) * NH, :, :], Zd[b].rearrange("s (h d) -> h s d", h=NH)).then_inc(zb_in, 16)
                    sp.dma_start(small[b * NH:(b + 1) * NH, 0:2], Gd[b].rearrange("s h -> h s")).then_inc(zb_in, 16)
                sp.dma_start(small[:, 2:3], layer(A["state_m"], l).rearrange("b h -> (b h)").rearrange("(q a) -> q a", a=1)).then_inc(zb_in, 16)
                sp.dma_start(sv[:, 0, :], layer(A["state_n"], l).rearrange("b h k -> (b h) k")).then_inc(zb_in, 16)
                n_kv = 0
                for which, arr in (("k", "cache_win_k"), ("v", "cache_win_v")):
                    for b in range(NB):
                        s = n_kv % 3
                        if n_kv >= 3:
                            m = n_kv - 3
                            if m < NB:
                                sp.wait_ge(kq_used, m + 1)
                            else:
                                sp.wait_ge(v_used, m - NB + 1)
                        ztf = zt[:, :, :].rearrange("p t c -> p (t c)")
                        kv = ztf[:, s * 1536:(s + 1) * 1536].rearrange("p (r c) -> p r c", r=3)
                        src = layer(A[arr], l)[b].rearrange("w h d -> w (h d)")
                        for r, (win, dil) in enumerate(DIL):
                            g = src[PAST - win:PAST, :].rearrange("(j r) c -> j r c", r=dil)[:, 0, :]
                            sp.dma_start(kv[:, r, :], g).then_inc(kv_in[s], 16)
                        if which == "k":
                            if b >= 2:
                                sp.wait_ge(kq_used, b - 1)
                            qd = (att[:, 1536:2048], att[:, 2048:2560])[b % 2]
                            sp.dma_start(qd, Zd[b, 0:1, :].to_broadcast([P, WA])).then_inc(q_in[b % 2], 16)
                        n_kv += 1
                sp.wait_ge(so_done, 1)
                sp.dma_start(Ad, yb[0:NB, 0:4, :].rearrange("p t c -> p (t c)")).then_inc(as_stored, 16)
                sp.wait_ge(as_stored, 16)
                sp.dma_start(sv[:, 3, :], Ad.rearrange("b (h d) -> (b h) d", d=HD)).then_inc(as_in, 16)
                sp.wait_ge(v_used, NB)
                ztf = zt[:, :, :].rearrange("p t c -> p (t c)")
                sp.dma_start(ztf[0:HD, 0:4096], layer(A["state_C"], l).rearrange("b h v k -> (b h) (v k)")).then_inc(cst_in, 16)
                sp.wait_ge(ys_done, 1)
                ysv = Yd[SEQ:TOK, :].rearrange("b (h d) -> b h d", d=HD)
                for b in range(NB):
                    r = slice(b * NH, (b + 1) * NH)
                    sp.dma_start(ysv[b, 0:NH, :], sv[r, 3, :]).then_inc(ys_stored, 16)
                    sp.dma_start(ysv[b, NH:2 * NH, :], sv[r, 2, :]).then_inc(ys_stored, 16)
                sp.dma_start(Hd.rearrange("b (h d) -> (b h) d", d=HD), sv[:, 1, :]).then_inc(ys_stored, 16)
                sp.dma_start(layer(O["C_s"], l).rearrange("b h v k -> (b h) (v k)"), ztf[0:HD, 0:4096]).then_inc(cst_out, 16)
                sp.dma_start(layer(O["n_s"], l).rearrange("b h k -> (b h) k"), sv[:, 0, :]).then_inc(cst_out, 16)
                sp.dma_start(layer(O["m_s"], l).rearrange("b h -> (b h)").rearrange("(q a) -> q a", a=1), small[:, 3:4]).then_inc(cst_out, 16)
                sp.wait_ge(ys_stored, 16 * 17)
                sp.wait_ge(cst_out, 48)
                sp.wait_ge(c_stored, 48 * PAIRS)
                sp.dma_start(yb[0:NB, 0:4, :].rearrange("p t c -> p (t c)"), Hd).then_inc(ys_in, 16)
                sp.dma_start(att[0:NB, 2048:3072], Yd[SEQ:TOK, :]).then_inc(ys_in, 16)
                for h, name in enumerate(("out_norm_a", "out_norm_b")):
                    sp.dma_start(rowr[:, h * WA:(h + 1) * WA], A[name][bass.ds(l, 1), :].to_broadcast([P, WA])).then_inc(ygain_in, 16)
                for t in range(NT + 1):
                    if t >= 2:
                        sp.wait_ge(yt_ready, t - 1)
                    sp.dma_start(att[0:rows(t), (t % 2) * D:(t % 2 + 1) * D], Yd[tok(t), :]).then_inc(yst_in[t % 2], 16)
                    if t == 0:
                        sp.wait_ge(ssq_done, 1)
                        sp.dma_start(X[:, :, :], Xd).then_inc(x_back, 16)
                load_block(l, B_FFN + 2)
                with sp.Fori(1, FG) as i:
                    for j in range(3):
                        n = B_FFN + 3 + j
                        sp.wait_ge(w_split, n - 3 + 1 + (i - 1) * 3)
                        for dst, src in weight_sources(l, n, i):
                            sp.dma_start(dst, src).then_inc(raw_in[n % NSLOT], 16)
                for n in range(B_PLE, B_PLE + 4):
                    load_block(l, n)
                for t in range(NT + 1):
                    if t >= 2:
                        sp.wait_ge(pt_ready, t - 1)
                    else:
                        sp.wait_ge(dn_read, 24 * FG)
                    src = layer(A["p_prompt"], l).rearrange("z s e -> (z s) e")[tok(t), :] if t < NT else \
                        layer(A["p_sample"], l).rearrange("b z e -> b (z e)")
                    sp.dma_start(wb[0:rows(t), (t % 2) * 512:(t % 2) * 512 + PLE], src).then_inc(pst_in[t % 2], 16)
                for n in range(B_PLE + 4, B_PLE + 8):
                    load_block(l, n)
                for g in range(3):
                    w = min(8, FT - 8 * g) * P
                    sp.wait_ge(tl_done, g + 1)
                    src = (wa, wb)[g % 2]
                    fs = slice(8 * g * P, 8 * g * P + w)
                    sp.dma_start(layer(O["conv_p"], l).rearrange("z j f -> (z j) f")[:, fs], src[0:2, 0:w]).then_inc(tl_stored, 16)
                    sp.dma_start(layer(O["conv_s"], l)[:, 1, fs], src[2:2 + NB, 0:w]).then_inc(tl_stored, 16)
                sp.wait_ge(tl_stored, 96)
                sp.wait_ge(cs_copied, 16)
                sp.wait_ge(engines_done, 4 * l + 4)
                sp.sem_inc(settled, 1)
                for s in layer_sems:
                    sp.sem_clear(s)
                sp.sem_inc(layer_open, 1)
            for t in range(NT + 1):
                sp.wait_ge(fin_evac_a, t + 1)
                sp.wait_ge(fin_evac_v, t + 1)
                dst = O["y_p"][0, tok(t), :] if t < NT else O["y_s"][:, 0, :]
                stage = (wa, wb)[t % 2]
                sp.dma_start(dst, stage[0:rows(t), 0:D]).then_inc(y_stored[t % 2], 16)
            sp.wait_ge(y_stored[0], 16 * 5)
            sp.wait_ge(y_stored[1], 16 * 4)

        def end_layer(eng, l):
            eng.drain().then_inc(engines_done, 1)
            eng.wait_ge(layer_open, l + 1)

        @block.gpsimd
        def _(pool):
            def split(n, later=0, freed=None):
                s, used = n % NSLOT, BLOCKS[n][3]
                pool.wait_ge(raw_in[s], raw_value(n) + 16 * later)
                if n >= NSLOT:
                    pool.wait_ge(gemm_done, BLOCKS[n - NSLOT][4] + 36 * later)
                pool.tensor_tensor(out=whi[:, s, 0:used], in0=raw[:, s, 0:used],
                                   in1=ones[:, 0:1].to_broadcast([P, used]), op=ALU.mult).then_inc(pool_step, 1)
                pool.wait_ge(pool_step, n + 1 + 3 * later)
                pool.tensor_tensor(out=wlo[:, s, 0:used], in0=raw[:, s, 0:used],
                                   in1=whi[:, s, 0:used].bitcast(F32), op=ALU.subtract).then_inc(w_split, 1)

            pool.memset(ones[:, :], 1.0).then_inc(const_set, 1)
            pool.memset(eps[:, :], EPS).then_inc(const_set, 1)
            pool.memset(one1[:, :], 1.0).then_inc(const_set, 1)
            pool.memset(gz[:, :, :], 0.0).then_inc(const_set, 1)
            pool.memset(ssq[:, :], 1.0).then_inc(const_set, 1)
            pool.memset(rcol[:, :], 1.0).then_inc(const_set, 1)
            pool.wait_ge(const_set, 6)
            with pool.Fori(0, DEPTH) as l:
                for n in range(B_FFN + 3):
                    split(n)
                with pool.Fori(0, FG - 1) as i:
                    for j in range(3):
                        split(B_FFN + 3 + j, i)
                for n in range(B_PLE, B_PLE + 8):
                    split(n)
                end_layer(pool, l)

        @block.tensor
        def _(pe):
            def three(out, a_hi, a_lo, b_hi, b_lo, first, last):
                nc.tensor.matmul(out, a_lo, b_hi, start=first, stop=False)
                nc.tensor.matmul(out, a_hi, b_lo, start=False, stop=False)
                return nc.tensor.matmul(out, a_hi, b_hi, start=False, stop=last)

            def weights(n, k, width, at, cols):
                s = n % NSLOT
                r = slice(k * width + at, k * width + at + cols)
                return whi[:, s, r], wlo[:, s, r]

            def sums(i):
                pe.wait_ge(sq_used, KT * (i + 1))
                for c in range(3):
                    mm = nc.tensor.matmul(ps[:, 5 + c, 0:CH], ones[:, :], wa[:, col(c)], start=True, stop=True)
                mm.then_inc(ss_ready, 1)

            def in_tile(p, t):
                i = p * (NT + 1) + t
                width = (3 if p < PAIRS else 4) * P
                if i >= 4:
                    pe.wait_ge(z_done, i - 3)
                if t == 0:
                    pe.wait_ge(w_split, B_IN + 2 * p + 1)
                out = ps[0:rows(t), i % 4, 0:width]
                for k in range(KT):
                    if t == 0 and k == 4:
                        pe.wait_ge(w_split, B_IN + 2 * p + 2)
                    w_h, w_l = weights(B_IN + 2 * p + k // 4, k % 4, width, 0, width)
                    mm = three(out, hi[:, k, tok(t)], lo[:, k, tok(t)], w_h, w_l, k == 0, k == KT - 1)
                mm.then_inc(gemm_done, 1)

            def turn_qk():
                for j in range(4):
                    for x in range(4):
                        t = 4 * (j % 2) + x
                        mm = nc.tensor.transpose(ps[:, 4 + j, x * P:(x + 1) * P],
                                                 zt[:, t, (j // 2) * P:(j // 2 + 1) * P], ident[:, :])
                    mm.then_inc(turned, 1)

            pe.wait_ge(const_in, 32)
            for t in range(NT + 1):
                m = rows(t)
                pe.wait_ge(x_in[t % 2], 16 * (t // 2 + 1))
                if t >= 2:
                    pe.wait_ge(x_evac_a, t - 1)
                    pe.wait_ge(x_evac_v, t - 1)
                for k in range(KT):
                    mm = nc.tensor.transpose(ps[:, 2 * (t % 2) + k // 4, (k % 4) * m:(k % 4 + 1) * m],
                                             (wa, wb)[t % 2][0:m, k * P:(k + 1) * P], ident[0:m, 0:m])
                mm.then_inc(x_turned, 1)
            pe.wait_ge(x_evac_a, NT + 1)
            pe.wait_ge(x_evac_v, NT + 1)
            pe.wait_ge(const_set, 6)

            with pe.Fori(0, DEPTH) as l:
                pe.wait_ge(gst_in, 48)
                nc.tensor.transpose(ps[:, 0, 0:3 * KT], gst[:, :], ident[0:3 * KT, 0:3 * KT]).then_inc(gst_t, 1)
                pe.wait_ge(cs_in, 48)
                nv = 2 * NB + CW + 1
                for f in range(FT):
                    mm = nc.tensor.transpose(ps[:, 1, f * nv:(f + 1) * nv], att[0:nv, f * P:(f + 1) * P], ident[0:nv, 0:nv])
                mm.then_inc(cs_t, 1)
                pe.wait_ge(w_split, 1)
                for t in range(NT + 1):
                    out = ps[0:rows(t), 4, t * 2 * NH:(t + 1) * 2 * NH]
                    for k in range(KT):
                        if t == 0:
                            pe.wait_ge(split_lo, k + 1)
                        w_h, w_l = weights(0, k, 2 * NH, 0, 2 * NH)
                        mm = three(out, hi[:, k, tok(t)], lo[:, k, tok(t)], w_h, w_l, k == 0, k == KT - 1)
                mm.then_inc(gemm_done, 1)
                sums(0)
                pe.wait_ge(gains_done, 1)
                pe.wait_ge(cvec_done, 1)
                for p in range(2 * PAIRS):
                    for t in range(NT + 1):
                        if p == 0 and t == 2:
                            pe.wait_ge(rstd_done, 1)
                            for x in range(NT + 1):
                                mm = nc.tensor.matmul(ps[0:rows(x), 5, x:x + 1], rstd[0:1, tok(x)], ident[0:1, 0:1],
                                                      start=True, stop=True)
                            mm.then_inc(rcol_ready, 1)
                        if p >= 1 and t == 0:
                            if p <= PAIRS:
                                pe.wait_ge(s_masked, 16 * p)
                            else:
                                pe.wait_ge(n_read, NT * (p - PAIRS))
                                pe.wait_ge(sc_done, NT * (p - PAIRS))
                        in_tile(p, t)
                    if p == 0:
                        pe.wait_ge(gates_read, 1)
                        pe.wait_ge(rcol_done, 1)
                    if p < PAIRS:
                        pe.wait_ge(qk_norm, p + 1)
                        if p >= 1:
                            pe.wait_ge(o_read, 16 * p)
                    else:
                        pe.wait_ge(z_done, (NT + 1) * (p + 1))
                        if p == PAIRS:
                            pe.wait_ge(o_read, 16 * p)
                            for j in range(4):
                                for x in range(4):
                                    t = 4 * (j % 2) + x
                                    mm = nc.tensor.transpose(ps[0:NH, 4 + j, x * P:(x + 1) * P],
                                                             gz[:, t, (j // 2) * NH:(j // 2 + 1) * NH], ident[:, :])
                            mm.then_inc(gr_ready, 1)
                            pe.wait_ge(rows_done, 1)
                            for c in range(NT):
                                nc.tensor.transpose(ps[:, 4, c * NH:(c + 1) * NH], att[0:NH, c * P:(c + 1) * P],
                                                    ident[0:NH, 0:NH])
                                mm = nc.tensor.transpose(ps[:, 4, 64 + c * NH:64 + (c + 1) * NH],
                                                         att[0:NH, 3 * SEQ + c * P:3 * SEQ + (c + 1) * P], ident[0:NH, 0:NH])
                            mm.then_inc(gc_ready, 1)
                            pe.wait_ge(uc_done, 1)
                            pe.wait_ge(em_done, 1)
                        else:
                            pe.wait_ge(c_upd, 9 * (p - PAIRS))
                            pe.wait_ge(ct_done, p - PAIRS)
                            pe.wait_ge(rm_done, 2 * (p - PAIRS))
                    turn_qk()
                    pe.wait_ge(q_evac, 2 * (p + 1))
                    pe.wait_ge(k_evac, 2 * (p + 1))
                    pe.wait_ge(z_done, (NT + 1) * (p + 1))
                    if p < PAIRS:
                        def scores(u):
                            e, qb = UNITS[u]
                            g = 16 * p + u
                            if g >= 2:
                                pe.wait_ge(s_masked, g - 1)
                            n = (qb + 1) * P
                            r = slice(HD * e, HD * e + HD)
                            for a in range(0, n, 512):
                                w = min(512, n - a)
                                mm = nc.tensor.matmul(ps[:, 2 * (g % 2) + a // 512, 0:w], qT[r, qb * P:(qb + 1) * P],
                                                      kT[r, a:a + w], start=True, stop=True)
                            mm.then_inc(s_ready, 1)

                        def turn_p(u):
                            e, qb = UNITS[u]
                            g = 16 * p + u
                            pe.wait_ge(p_done, g + 1)
                            for half in range(qb // 4 + 1):
                                if half == 0 and g:
                                    pe.wait_ge(pt0, g)
                                if half == 1 and far(g):
                                    pe.wait_ge(pt1, far(g))
                                for kb in range(4 * half, min(qb + 1, 4 * half + 4)):
                                    mm = nc.tensor.transpose(ps[:, 4 + half, (kb % 4) * P:(kb % 4 + 1) * P],
                                                             att[:, (g % 2) * SEQ + kb * P:(g % 2) * SEQ + (kb + 1) * P],
                                                             ident[:, :])
                                mm.then_inc((t0_ready, t1_ready)[half], 1)

                        def values(u):
                            e, qb = UNITS[u]
                            g = 16 * p + u
                            pe.wait_ge(pt0, g + 1)
                            if far(g + 1):
                                pe.wait_ge(pt1, far(g + 1))
                            if g >= 2:
                                pe.wait_ge(o_read, g - 1)
                            at = VO + e * (HD + 1)
                            for kb in range(qb + 1):
                                a = 2 * SEQ + (g % 2) * SEQ + kb * P
                                mm = nc.tensor.matmul(ps[:, 6 + g % 2, 0:HD + 1], att[:, a:a + P], zt[:, kb, at:at + HD + 1],
                                                      start=(kb == 0), stop=(kb == qb))
                            mm.then_inc(o_ready, 1)

                        scores(0)
                        scores(1)
                        for u in range(16):
                            turn_p(u)
                            if u + 2 < 16:
                                scores(u + 2)
                            if u:
                                values(u - 1)
                        values(15)
                    else:
                        q = p - PAIRS
                        pe.wait_ge(iw_done, 1)
                        for j in range(2):
                            for e in range(2):
                                mm = nc.tensor.matmul(ps[HD * e:HD * e + HD, 4 + j, :], sel[:, 2 * q + e, 0:HD],
                                                      rowi[:, j * 512:(j + 1) * 512], start=True, stop=True)
                        mm.then_inc(ib_ready, 1)
                        for e in range(2):
                            if e == 1:
                                pe.wait_ge(ib_used, q + 1)
                            for j in range(2):
                                mm = nc.tensor.matmul(ps[:, (6, 4)[e] + j, :], sel[:, 2 * q + e, :],
                                                      rowr[0:NH, j * 512:(j + 1) * 512], start=True, stop=True)
                            mm.then_inc(rb_ready, 1)

                        def kq(c):
                            g = NT * q + c
                            if g >= 2:
                                pe.wait_ge(sc_done, g - 1)
                            for e in range(2):
                                r = slice(HD * e, HD * e + HD)
                                mm = nc.tensor.matmul(ps[:, (0, 6)[c % 2] + e, 0:P], kT[r, c * P:(c + 1) * P],
                                                      qT[r, c * P:(c + 1) * P], start=True, stop=True)
                            mm.then_inc(a_ready, 1)

                        kq(0)
                        pe.wait_ge(rm_done, 2 * (q + 1))
                        for c in range(NT):
                            g = NT * q + c
                            if c + 1 < NT:
                                kq(c + 1)
                            pe.wait_ge(ws_done, g + 1)
                            mm = nc.tensor.matmul(ps[:, 4 + c % 2, 0:2 * (HD + 1)],
                                                  att[:, 3 * SEQ + 512 + (c % 2) * P:3 * SEQ + 512 + (c % 2 + 1) * P],
                                                  zt[:, c, VO:OG], start=True, stop=True)
                            mm.then_inc(u_ready, 1)
                            pe.wait_ge(sc_done, g + 1)
                            if g >= 2:
                                pe.wait_ge(n_read, g - 1)
                            for e in range(2):
                                at = VO + e * (HD + 1)
                                a = 3 * SEQ + (c % 2) * 256 + e * P
                                nc.tensor.matmul(ps[:, 2 + c % 2, e * (HD + 1):(e + 1) * (HD + 1)], att[:, a:a + P],
                                                 zt[:, c, at:at + HD + 1], start=(e == 0), stop=False)
                            pe.wait_ge(c_upd, 9 * q + c + 1)
                            nc.tensor.matmul(ps[:, 2 + c % 2, 0:2 * (HD + 1)], att[:, 2 * SEQ + c * P:2 * SEQ + (c + 1) * P],
                                             Cst[:, :], start=False, stop=True).then_inc(n_ready, 1)
                        pe.wait_ge(c_upd, 9 * (q + 1))
                        for e in range(2):
                            mm = nc.tensor.transpose(ps[0:HD, 6, e * P:(e + 1) * P], Cst[:, e * (HD + 1):e * (HD + 1) + HD], ident[:, :])
                        mm.then_inc(ct_ready, 1)

                pe.wait_ge(s_scores, 1)
                for r in range(3):
                    mm = nc.tensor.transpose(ps[0:HD, 0, r * P:(r + 1) * P], att[:, 2560 + r * HD:2560 + (r + 1) * HD], ident[:, :])
                mm.then_inc(st_ready, 1)
                pe.wait_ge(pj_ready, 1)
                for r in range(3):
                    mm = nc.tensor.transpose(ps[:, 1, r * HD:(r + 1) * HD], att[0:HD, 3072 + r * P:3072 + (r + 1) * P],
                                             ident[0:HD, 0:HD])
                mm.then_inc(pj_back, 1)
                pe.wait_ge(pj_done, 1)
                ztf = zt[:, :, :].rearrange("p t c -> p (t c)")
                for b in range(NB):
                    m = NB + b
                    s = m % 3
                    pe.wait_ge(kv_in[s], 48 * (m // 3 + 1))
                    for c in range(4):
                        for r in range(3):
                            a = s * 1536 + r * WA + c * P
                            mm = nc.tensor.matmul(ps[:, 2, c * 64 + b * NH:c * 64 + (b + 1) * NH], ztf[:, a:a + P],
                                                  att[:, 3584 + r * HD + b * NH:3584 + r * HD + (b + 1) * NH],
                                                  start=(r == 0), stop=(r == 2))
                    mm.then_inc(v_used, 1)
                pe.wait_ge(ot_done, 1)
                for c in range(4):
                    mm = nc.tensor.transpose(ps[0:NB, 3, c * P:(c + 1) * P], att[:, 2048 + c * NB:2048 + (c + 1) * NB], ident[:, :])
                mm.then_inc(so_ready, 1)

                pe.wait_ge(so_done, 1)
                pe.wait_ge(ct_done, PAIRS)
                for t in range(NT + 1):
                    m = rows(t)
                    pe.wait_ge(yn_done, t + 1)
                    if t >= 2:
                        pe.wait_ge(yh_done, 2 * (t - 1))
                        pe.wait_ge(yl_done, 2 * (t - 1))
                    for k in range(KT):
                        mm = nc.tensor.transpose(ps[:, 2 * (t % 2) + k // 4, (k % 4) * m:(k % 4 + 1) * m],
                                                 att[0:m, (t % 2) * D + k * P:(t % 2) * D + (k + 1) * P], ident[0:m, 0:m])
                    mm.then_inc(yt_ready, 1)
                pe.wait_ge(yl_done, 2 * (NT + 1))
                for b in range(4):
                    pe.wait_ge(w_split, B_OUT + b + 1)
                    for c in range(3):
                        for o in range(2):
                            j = 6 * b + 2 * c + o
                            if j >= 4:
                                pe.wait_ge(wo_done, j - 3)
                            for k in range(KT):
                                w_h, w_l = weights(B_OUT + b, k, 256, o * P, P)
                                mm = three(ps[:, 4 + j % 4, 0:CH], w_h, w_l, hi[:, k, col(c)], lo[:, k, col(c)], k == 0, k == KT - 1)
                            mm.then_inc(gemm_done, 1)

                def group(i, first):
                    for o in range(2):
                        for kind in range(2):
                            n = B_FFN + kind
                            if o == 0:
                                pe.wait_ge(w_split, n + 1 + 3 * i)
                            for c in range(3):
                                if first and o == 0 and kind == 0 and c == 2:
                                    sums(1)
                                if kind == 0:
                                    if not (first and o == 0):
                                        pe.wait_ge(gate_read, 6 * i + 3 * o - 3 + c + 1)
                                elif not (first and o == 0 and c < 2):
                                    pe.wait_ge(y_val, 6 * i + 3 * o + c - 2 + 1)
                                bank = c if kind == 0 else 3 + (3 * o + c) % 2
                                for k in range(KT):
                                    if first and (o, kind, c) == (0, 0, 0):
                                        pe.wait_ge(split_lo, KT + k + 1)
                                    w_h, w_l = weights(n, k, 256, o * P, P)
                                    mm = three(ps[:, bank, 0:CH], w_h, w_l, hi[:, k, col(c)], lo[:, k, col(c)], k == 0, k == KT - 1)
                                mm.then_inc(gemm_done, 1)
                    n = B_FFN + 2
                    pe.wait_ge(w_split, n + 1 + 3 * i)
                    for c in range(3):
                        pe.wait_ge(y_lo, 6 * i + 3 + c + 1)
                        for o in range(KT):
                            j = 8 * c + o
                            if not (first and j < 3):
                                pe.wait_ge(dn_read, 24 * i + j - 3 + 1)
                            for k in range(2):
                                w_h, w_l = weights(n, k, D, o * P, P)
                                mm = three(ps[:, 5 + j % 3, 0:CH], w_h, w_l, yhi[:, k, col(c)], ylo[:, k, col(c)], k == 0, k == 1)
                            mm.then_inc(gemm_done, 1)

                pe.wait_ge(wo_done, 24)
                group(0, True)
                with pe.Fori(1, FG) as i:
                    group(i, False)
                pe.wait_ge(y_val, 6 * FG)
                pe.wait_ge(dn_read, 24 * FG)
                for t in range(NT + 1):
                    m = rows(t)
                    pe.wait_ge(pst_in[t % 2], 16 * (t // 2 + 1))
                    if t >= 2:
                        pe.wait_ge(pt_lo, t - 1)
                    for k in range(2):
                        mm = nc.tensor.transpose(ps[:, t % 2, k * m:(k + 1) * m], wb[0:m, (t % 2) * 512 + k * P:(t % 2) * 512 + (k + 1) * P], ident[0:m, 0:m])
                    mm.then_inc(pt_ready, 1)
                pe.wait_ge(pt_lo, NT + 1)
                for b in range(4):
                    pe.wait_ge(w_split, B_PLE + 2 * b + 2)
                    for c in range(3):
                        for o in range(2):
                            j = 6 * b + 2 * c + o
                            if j >= 3:
                                pe.wait_ge(pg_sc, j - 2)
                            for k in range(KT):
                                if j == 0:
                                    pe.wait_ge(split_lo, 2 * KT + k + 1)
                                w_h, w_l = weights(B_PLE + 2 * b, k, 256, o * P, P)
                                mm = three(ps[:, j % 3, 0:CH], w_h, w_l, hi[:, k, col(c)], lo[:, k, col(c)], k == 0, k == KT - 1)
                            mm.then_inc(gemm_done, 1)
                            if j >= 2:
                                pe.wait_ge(ple_done, j - 1)
                            for k in range(2):
                                w_h, w_l = weights(B_PLE + 2 * b + 1, k, 256, o * P, P)
                                mm = three(ps[:, 3 + j % 2, 0:CH], w_h, w_l, yhi[:, k, col(c)], ylo[:, k, col(c)], k == 0, k == 1)
                            mm.then_inc(gemm_done, 1)
                        if b == 0 and c == 0:
                            sums(2)
                pe.wait_ge(rstd_done, 3)
                pe.wait_ge(ple_done, 24)
                for g in range(3):
                    for f in range(8 * g, min(8 * g + 8, FT)):
                        mm = nc.tensor.transpose(ps[0:2 + NB, 2 * g + (f % 8) // 4, (f % 4) * P:(f % 4 + 1) * P],
                                                 tail[:, f, :], ident[:, :])
                    mm.then_inc(tl_ready, 1)
                end_layer(pe, l)
            for t in range(NT + 1):
                m = rows(t)
                if t >= 2:
                    pe.wait_ge(fin_evac_a, t - 1)
                    pe.wait_ge(fin_evac_v, t - 1)
                for k in range(KT):
                    mm = nc.tensor.transpose(ps[0:m, 2 * (t % 2) + k // 4, (k % 4) * P:(k % 4 + 1) * P], X[:, k, tok(t)], ident[:, :])
                mm.then_inc(fin_turned, 1)

        @block.scalar
        def _(act):
            do0 = Steps(act, act_step0)

            def act_split(do, i):
                for k in range(KT):
                    n = KT * i + k
                    do(nc.scalar.activation(hi[:, k, :], X[:, k, :], ACT.Identity, scale=gains[:, n:n + 1]), split_hi, wait=False)
                    if k >= 2:
                        act.wait_ge(sq_used, n - 1)
                    do(nc.scalar.activation(sq[:, k % 2, :], X[:, k, :], ACT.Square), sq_ready)

            def act_rstd(do, i):
                act.wait_ge(ss_ready, i + 1)
                for c in range(3):
                    do(nc.scalar.activation(rstd[:, col(c)], ps[:, 5 + c, 0:CH], ACT.Ln, scale=1.0 / D, bias=eps[:, :]))
                do(nc.scalar.activation(rstd[:, :], rstd[:, :], ACT.Exp, scale=-0.5), rs_first)

            act.wait_ge(const_set, 6)
            for t in range(NT + 1):
                m = rows(t)
                act.wait_ge(x_turned, t + 1)
                do0(nc.scalar.activation(X[:, 0:4, tok(t)], ps[:, 2 * (t % 2), 0:4 * m].rearrange("p (k m) -> p k m", k=4), ACT.Copy), x_evac_a)
            act.wait_ge(x_evac_v, NT + 1)
            with act.Fori(0, DEPTH) as l:
                do = Steps(act, act_step)
                act.wait_ge(gains_done, 1)
                act_split(do, 0)
                act_rstd(do, 0)
                act.wait_ge(gz_abs, 1)
                do(nc.scalar.activation(gt[:, :, :], gt[:, :, :], ACT.Exp, scale=-1.0))
                do(nc.scalar.activation(gt[:, :, :], gt[:, :, :], ACT.Ln, bias=one1[:, :]), gz_ln)
                act.wait_ge(rcol_done, 1)
                act.wait_ge(x_spilled, 16)
                for p in range(2 * PAIRS):
                    if p:
                        if p <= PAIRS:
                            act.wait_ge(o_ready, 16 * p)
                            act.wait_ge(z_stored, 16 * 8 * p)
                        else:
                            act.wait_ge(n_ready, NT * (p - PAIRS))
                            act.wait_ge(u_ready, NT * (p - PAIRS))
                            act.wait_ge(z_stored, 16 * (8 * PAIRS + 4 * (p - PAIRS)))
                            act.wait_ge(yb_done, p)
                    for t in range(NT + 1):
                        i = p * (NT + 1) + t
                        m = rows(t)
                        act.wait_ge(gemm_done, GEMM_IN + i + 1)
                        z = ps[0:m, i % 4, :]
                        r = rcol[0:m, t:t + 1]
                        do(nc.scalar.activation(zt[0:m, t, 0:2 * P], z[:, 0:2 * P], ACT.Identity, scale=r), wait=False)
                        if p >= PAIRS:
                            do(nc.scalar.activation(zt[0:m, t, OG:ZW], z[:, 3 * P:4 * P], ACT.Identity, scale=r), wait=False)
                        v = zt[0:m, t, VO:OG].rearrange("p (e d) -> p e d", e=2)[:, :, 0:HD]
                        do(nc.scalar.activation(v, z[:, 2 * P:3 * P].rearrange("p (e d) -> p e d", e=2), ACT.Identity, scale=r), z_done)
                        if p < PAIRS and t in (6, NT):
                            half = int(t == NT)
                            hc = slice(16 * half, 16 if half == 0 else 4 * (NT + 1))
                            act.wait_ge(qk_ssq, 2 * p + half + 1)
                            do(nc.scalar.activation(qs36[:, 1, hc], qs36[:, 0, hc], ACT.Ln, scale=1.0 / HD, bias=eps[:, :]))
                            do(nc.scalar.activation(qs36[:, 1, hc], qs36[:, 1, hc], ACT.Exp, scale=-0.5), qk_rs)
                    if p == PAIRS:
                        act.wait_ge(r2_done, 1)
                        do(nc.scalar.activation(rowi[:, :], rowi[:, :], ACT.Exp), iw_done)
                        act.wait_ge(gc_ready, 1)
                        act.wait_ge(uc_done, 1)
                        do(nc.scalar.activation(em[:, :, :], ps[:, 4, 64:128].rearrange("p (c h) -> p c h", c=NT), ACT.Exp, scale=-1.0), em_done)
                    for j in range(2):
                        act.wait_ge(turned, 4 * p + j + 1)
                        do(nc.scalar.activation(qT[:, j * 512:(j + 1) * 512], ps[:, 4 + j, :], ACT.Copy), q_evac)
                    if p >= PAIRS:
                        do(nc.scalar.activation(zt[:, 0:NT, OG:ZW], zt[:, 0:NT, OG:ZW], ACT.Exp, scale=-1.0))
                        do(nc.scalar.activation(zt[0:NB, NT, OG:ZW], zt[0:NB, NT, OG:ZW], ACT.Exp, scale=-1.0), o_exp)
                    if p < PAIRS:
                        def evac_far(u):
                            g = 16 * p + u
                            if UNITS[u][1] >= 4:
                                act.wait_ge(t1_ready, far(g + 1))
                                if g >= 2:
                                    act.wait_ge(o_ready, g - 1)
                                n = (UNITS[u][1] - 3) * P
                                a = 2 * SEQ + (g % 2) * SEQ + 512
                                do(nc.scalar.activation(att[:, a:a + n], ps[:, 5, 0:n], ACT.Copy), pt1)

                        for u in range(16):
                            g = 16 * p + u
                            n = (UNITS[u][1] + 1) * P
                            act.wait_ge(s_masked, g + 1)
                            s = att[:, (g % 2) * SEQ:(g % 2) * SEQ + n]
                            do(nc.scalar.activation(s, s, ACT.Exp, scale=SCALE, bias=nm[:, g % 2:g % 2 + 1]), p_done)
                            evac_far(u)
                    else:
                        q = p - PAIRS
                        for e in range(2):
                            act.wait_ge(rm_done, 2 * q + e + 1)
                            for c in range(NT):
                                d = att[:, e * SEQ + c * P:e * SEQ + (c + 1) * P]
                                h = 2 * q + e
                                do(nc.scalar.activation(d, d, ACT.Exp, bias=uc[:, c, h:h + 1]), d_done, wait=False)
                act.wait_ge(sp_max, 1)
                do(nc.scalar.activation(att[0:HD, 3072:3072 + 385], att[0:HD, 3072:3072 + 385], ACT.Exp, scale=SCALE,
                                        bias=small[:, 10:11], accum_out=small[:, 11:12]), sp_exp)
                act.wait_ge(sc_exp_in, 1)
                do(nc.scalar.activation(small[:, 7:10], small[:, 7:10], ACT.Exp), sc_exp)
                act.wait_ge(ssq_done, 1)
                do(nc.scalar.activation(yrs[:, :], ssq[:, :], ACT.Ln, scale=1.0 / WA, bias=eps[:, :]))
                do(nc.scalar.activation(yrs[:, :], yrs[:, :], ACT.Exp, scale=-0.5), yrs_first)
                for t in range(NT + 1):
                    m = rows(t)
                    act.wait_ge(yt_ready, t + 1)
                    for j in range(2):
                        z = ps[:, 2 * (t % 2) + j, 0:4 * m].rearrange("p (k m) -> p k m", k=4)
                        do(nc.scalar.activation(hi[:, 4 * j:4 * j + 4, tok(t)], z, ACT.Copy), yh_done)
                act.wait_ge(wo_done, 24)
                act_split(do, 1)
                act_rstd(do, 1)

                def conv_tile(i, o):
                    f = 2 * i + o
                    act.wait_ge(conv_1, 2 * i + o + 1)
                    do(nc.scalar.activation(wb[:, :], wb[:, :], ACT.Gelu_apprx_tanh), gelu_done)
                    for c in range(3):
                        act.wait_ge(y_val, 6 * i + 3 * o + c + 1)
                        if o == 0 and c == 0:
                            pass
                        do(nc.scalar.activation(yhi[:, o, col(c)], wb[:, col(c)], ACT.Copy), y_hi)

                with act.Fori(0, FG) as i:
                    do.loop(i, {gelu_done: 2, y_hi: 6})
                    for o in range(2):
                        conv_tile(i, o)
                    do.end_loop(FG)
                act.wait_ge(dn_read, 24 * FG)
                act_split(do, 2)
                for t in range(NT + 1):
                    m = rows(t)
                    act.wait_ge(pt_ready, t + 1)
                    z = ps[:, t % 2, 0:2 * m].rearrange("p (k m) -> p k m", k=2)
                    do(nc.scalar.activation(yhi[:, :, tok(t)], z, ACT.Copy), pt_hi)
                act_rstd(do, 2)
                for j in range(24):
                    c = (j % 6) // 2
                    act.wait_ge(pg_sc, j + 1)
                    do(nc.scalar.activation(wa[:, col(j % 3)], wa[:, col(j % 3)], ACT.Exp, scale=-1.0), pg_exp)
                end_layer(act, l)
            for t in range(NT + 1):
                m = rows(t)
                act.wait_ge(fin_turned, t + 1)
                if t >= 2:
                    act.wait_ge(y_stored[t % 2], 16 * (t // 2))
                do0(nc.scalar.activation((wa, wb)[t % 2][0:m, 0:512], ps[0:m, 2 * (t % 2), :], ACT.Copy), fin_evac_a)

        @block.vector
        def _(dve):
            v = nc.vector
            do0 = Steps(dve, dve_step0)

            def dve_split(do, i):
                for k in range(KT):
                    n = KT * i + k
                    dve.wait_ge(split_hi, n + 1)
                    do(v.scalar_tensor_tensor(out=lo[:, k, :], in0=X[:, k, :], scalar=gains[:, n:n + 1],
                                              in1=hi[:, k, :].bitcast(F32), op0=ALU.mult, op1=ALU.subtract), split_lo, wait=False)
                    dve.wait_ge(sq_ready, n + 1)
                    if k == 0:
                        do(v.tensor_copy(wa[:, 0:TOK], sq[:, k % 2, :]), sq_used)
                    else:
                        do(v.tensor_tensor(out=wa[:, 0:TOK], in0=wa[:, 0:TOK], in1=sq[:, k % 2, :], op=ALU.add), sq_used)

            def newton(do, y, tmp, sums_of, count, done):
                do(v.tensor_tensor(out=tmp, in0=y, in1=y, op=ALU.mult))
                for part, s in sums_of:
                    do(v.scalar_tensor_tensor(out=part(tmp), in0=s, scalar=count * EPS, in1=part(tmp), op0=ALU.add, op1=ALU.mult))
                do(v.tensor_scalar(tmp, tmp, -0.5 / count, 1.5, ALU.mult, ALU.add))
                do(v.tensor_tensor(out=y, in0=y, in1=tmp, op=ALU.mult), done)

            def dve_rstd(do, i):
                dve.wait_ge(rs_first, i + 1)
                newton(do, rstd[:, :], wb[:, :],
                       [((lambda x, c=c: x[:, col(c)]), ps[:, 5 + c, 0:CH]) for c in range(3)], D, rstd_done)

            for t in range(NT + 1):
                m = rows(t)
                dve.wait_ge(x_turned, t + 1)
                do0(v.tensor_copy(X[:, 4:8, tok(t)], ps[:, 2 * (t % 2) + 1, 0:4 * m].rearrange("p (k m) -> p k m", k=4)), x_evac_v)
            dve.wait_ge(x_evac_a, NT + 1)
            dve.wait_ge(const_set, 6)
            with dve.Fori(0, DEPTH) as l:
                do = Steps(dve, dve_step)
                dve.wait_ge(gst_t, 1)
                do(v.tensor_copy(gains[:, :], ps[:, 0, 0:3 * KT]), gains_done)
                dve.wait_ge(cs_t, 1)
                do(v.tensor_copy(cvec[:, :, :], ps[:, 1, 0:FT * 20].rearrange("p (f n) -> p f n", f=FT)), cvec_done)
                dve_split(do, 0)
                dve_rstd(do, 0)
                dve.wait_ge(rcol_ready, 1)
                do(v.tensor_copy(rcol[:, 0:NT], ps[:, 5, 0:NT]))
                do(v.tensor_copy(rcol[0:NB, NT:NT + 1], ps[0:NB, 5, NT:NT + 1]), rcol_done)
                dve.wait_ge(vec_in, 16 * 8)
                for t in range(NT + 1):
                    m = rows(t)
                    do(v.scalar_tensor_tensor(out=gz[0:m, t, :], in0=ps[0:m, 4, t * 2 * NH:(t + 1) * 2 * NH], scalar=rcol[0:m, t:t + 1],
                                              in1=bgate[0:m, :], op0=ALU.mult, op1=ALU.add), gates_read if t == NT else None)
                f = gz[:, :, NH:2 * NH]
                do(v.scalar_tensor_tensor(out=gt[:, :, :], in0=f, scalar=-1.0, in1=f, op0=ALU.mult, op1=ALU.max), gz_abs)
                do(v.tensor_scalar(f, f, 0.0, None, ALU.min))
                dve.wait_ge(gz_ln, 1)
                do(v.tensor_tensor(out=f, in0=f, in1=gt[:, :, :], op=ALU.subtract), lf_done)
                dve.wait_ge(x_spilled, 16)
                ones_col = zt[:, :, VO:OG].rearrange("p t (e d) -> p t e d", e=2)[:, :, :, HD:HD + 1]
                do(v.memset(ones_col, 1.0))
                for p in range(2 * PAIRS):
                    h2 = p % PAIRS
                    if p:
                        dve.wait_ge(yb_stored, 16 * p)
                    if p < PAIRS:
                        s36 = qs36[:, 0, :].rearrange("p (t h) -> p t h", t=NT + 1)
                        r36 = qs36[:, 1, :].rearrange("p (t h) -> p t h", t=NT + 1)
                        if p == 0:
                            do(v.memset(qs36[:, 0, :], 1.0))
                        else:
                            dve.wait_ge(o_ready, 16 * p)
                        for half in range(2):
                            ts = slice(4 * half, 4 * half + 4)
                            parts = [(P, ts)] + ([(NB, slice(NT, NT + 1))] if half else [])
                            hc = slice(16 * half, 16 if half == 0 else 4 * (NT + 1))
                            dve.wait_ge(z_done, (NT + 1) * p + (4 if half == 0 else NT + 1))
                            for x, (m, w) in enumerate(parts):
                                n = w.stop - w.start
                                z2 = zt[0:m, w, 0:256]
                                sqv = att[0:m, 0:n * 256].rearrange("p (t c) -> p t c", t=n)
                                do(v.tensor_tensor(out=sqv, in0=z2, in1=z2, op=ALU.mult))
                                do(v.tensor_reduce(out=s36[0:m, w, :], in_=sqv.rearrange("p t (h d) -> p t h d", h=4), axis=AX.X, op=ALU.add),
                                   qk_ssq if x == len(parts) - 1 else None)
                            dve.wait_ge(qk_rs, 2 * p + half + 1)
                            newton(do, qs36[:, 1, hc], qs36[:, 2, hc], [((lambda x: x), qs36[:, 0, hc])], HD, None)
                            for m, w in parts:
                                n = w.stop - w.start
                                zz = zt[0:m, w, 0:256]
                                z4 = zz.rearrange("p t (h d) -> p t h d", h=4)
                                do(v.tensor_tensor(out=z4, in0=z4, in1=r36[0:m, w, :].unsqueeze(3).to_broadcast([m, n, 4, HD]), op=ALU.mult))
                                do(v.tensor_tensor(out=zz, in0=zz, in1=qkg[0:m, :, :].rearrange("p h d -> p (h d)").unsqueeze(1).to_broadcast([m, n, 256]), op=ALU.mult))
                                zr = z4[:, :, :, 0:2 * RH]
                                tmp = [att[0:m, j * 512:j * 512 + n * 64].rearrange("p (t h d) -> p t h d", t=n, h=4) for j in (0, 1)]
                                for j in (0, 1):
                                    cs = rope[0:m, w, 2 * RH * j:2 * RH * (j + 1)].unsqueeze(2).to_broadcast([m, n, 4, 2 * RH])
                                    do(v.tensor_tensor(out=tmp[j], in0=zr, in1=cs, op=ALU.mult))
                                do(v.tensor_tensor(out=zr[:, :, :, 0:RH], in0=tmp[0][:, :, :, 0:RH], in1=tmp[1][:, :, :, RH:], op=ALU.subtract))
                                do(v.tensor_tensor(out=zr[:, :, :, RH:], in0=tmp[0][:, :, :, RH:], in1=tmp[1][:, :, :, 0:RH], op=ALU.add),
                                   qk_norm if m == NB else None)
                    else:
                        q = p - PAIRS
                        if p == PAIRS:
                            ig, lf, bb, mm_ = [att[0:NH, j * SEQ:(j + 1) * SEQ] for j in range(4)]
                            dve.wait_ge(o_ready, 16 * PAIRS)
                            do(v.memset(rowi[:, :], 1.0))
                            do(v.memset(rowi[:, 0:SEQ:P], 0.0))
                            dve.wait_ge(gr_ready, 1)
                            for j in range(4):
                                do(v.tensor_copy(att[0:NH, j * 512:(j + 1) * 512], ps[0:NH, 4 + j, :]))
                            do(v.tensor_tensor_scan(out=bb, data0=rowi[:, :], data1=lf, initial=0.0, op0=ALU.mult, op1=ALU.add))
                            do(v.tensor_tensor_scan(out=mm_, data0=lf, data1=ig, initial=0.0, op0=ALU.add, op1=ALU.max))
                            do(v.memset(mprev[:, 0:1], 0.0))
                            do(v.tensor_copy(mprev[:, 1:NT], mm_[:, P - 1:SEQ - P:P]))
                            do(v.tensor_tensor(out=ig, in0=ig, in1=bb, op=ALU.subtract))
                            do(v.tensor_tensor(out=rowr[0:NH, :], in0=bb, in1=mm_, op=ALU.subtract), rows_done)
                            do(v.tensor_tensor(out=rowi[:, :].rearrange("p (c t) -> p c t", c=NT), in0=rowr[0:NH, :].rearrange("p (c t) -> p c t", c=NT),
                                               in1=mprev[:, :].unsqueeze(2).to_broadcast([NH, NT, P]), op=ALU.add), r2_done)
                            dve.wait_ge(gc_ready, 1)
                            do(v.tensor_copy(uc[:, :, :], ps[:, 4, 0:64].rearrange("p (c h) -> p c h", c=NT)), uc_done)
                            dve.wait_ge(mg_stored, 48)
                    for j in range(2):
                        dve.wait_ge(turned, 4 * p + 2 + j + 1)
                        do(v.tensor_copy(kT[:, j * 512:(j + 1) * 512], ps[:, 6 + j, :]), k_evac)
                    if p < PAIRS:
                        def masked(u):
                            e, qb = UNITS[u]
                            g = 16 * p + u
                            n = (qb + 1) * P
                            dve.wait_ge(s_ready, g + 1)
                            if g >= 2:
                                dve.wait_ge(t0_ready, g - 1)
                                if far(g - 1):
                                    dve.wait_ge(t1_ready, far(g - 1))
                            s = att[:, (g % 2) * SEQ:(g % 2) * SEQ + n]
                            src = ps[:, 2 * (g % 2):2 * (g % 2) + 2, :].rearrange("p b n -> p (b n)")[:, 0:n]
                            do(v.tensor_tensor_reduce(out=s, in0=src, in1=mask[:, SEQ - n:SEQ], scale=1.0, scalar=-3e38,
                                                      op0=ALU.add, op1=ALU.max, accum_out=den[:, 0:1]))
                            do(v.tensor_scalar(nm[:, g % 2:g % 2 + 1], den[:, 0:1], -SCALE, None, ALU.mult), s_masked)

                        def near(u):
                            e, qb = UNITS[u]
                            g = 16 * p + u
                            n = min(4, qb + 1) * P
                            dve.wait_ge(t0_ready, g + 1)
                            if g >= 2:
                                dve.wait_ge(o_ready, g - 1)
                            a = 2 * SEQ + (g % 2) * SEQ
                            do(v.tensor_copy(att[:, a:a + n], ps[:, 4, 0:n]), pt0)

                        def outputs(u):
                            e, qb = UNITS[u]
                            g = 16 * p + u
                            dve.wait_ge(o_ready, g + 1)
                            o = ps[:, 6 + g % 2, :]
                            do(v.reciprocal(den[:, 1:2], o[:, HD:HD + 1]))
                            do(v.tensor_scalar(yb[:, qb, e * HD:(e + 1) * HD], o[:, 0:HD], den[:, 1:2], None, ALU.mult), o_read)

                        masked(0)
                        masked(1)
                        for u in range(16):
                            near(u)
                            if u:
                                outputs(u - 1)
                            if u + 2 < 16:
                                masked(u + 2)
                        outputs(15)
                    else:
                        dve.wait_ge(ib_ready, q + 1)
                        iwb = ps[:, 4:6, :].rearrange("p b n -> p (b n)")
                        if q:
                            dve.wait_ge(n_ready, NT * q)
                            dve.wait_ge(c_stored, 48 * q)
                            dve.wait_ge(ct_ready, q)
                        do(v.tensor_copy(cwb[:, :], iwb[:, P - 1:SEQ:P]))
                        do(v.tensor_tensor(out=att[:, 2 * SEQ:3 * SEQ], in0=qT[:, :], in1=iwb, op=ALU.mult), ib_used)
                        for e in range(2):
                            dve.wait_ge(rb_ready, 2 * q + e + 1)
                            b0 = (6, 4)[e]
                            rb = ps[:, b0:b0 + 2, :].rearrange("p b (c t) -> p (b c) t", t=P)
                            do(v.tensor_tensor(out=att[:, e * SEQ:(e + 1) * SEQ].rearrange("p (c t) -> p c t", c=NT), in0=rb,
                                               in1=causal[:, :].unsqueeze(1).to_broadcast([P, NT, P]), op=ALU.add), rm_done)
                        do(v.memset(Cst[:, :], 0.0), c_upd)
                        dmat = att[:, 0:2 * SEQ].rearrange("p (e c t) -> p e c t", e=2, c=NT)
                        def prepare(c):
                            g = NT * q + c
                            dve.wait_ge(d_done, 2 * NT * q + NT + c + 1)
                            if g >= 2:
                                dve.wait_ge(u_ready, g - 1)
                                dve.wait_ge(n_ready, g - 1)
                            ws = att[:, 3 * SEQ + 512 + (c % 2) * P:3 * SEQ + 512 + (c % 2 + 1) * P].rearrange("p (e k) -> p e k", e=2)
                            kz = zt[:, c, P:2 * P].rearrange("p (e k) -> p e k", e=2)
                            do(v.scalar_tensor_tensor(out=ws, in0=kz, scalar=SCALE, in1=dmat[:, :, c, P - 1:P].to_broadcast([P, 2, HD]),
                                                      op0=ALU.mult, op1=ALU.mult), ws_done)
                            dve.wait_ge(a_ready, g + 1)
                            scs = att[:, 3 * SEQ + (c % 2) * 256:3 * SEQ + (c % 2 + 1) * 256].rearrange("p (e t) -> p e t", e=2)
                            do(v.scalar_tensor_tensor(out=scs, in0=ps[:, (0, 6)[c % 2]:(0, 6)[c % 2] + 2, 0:P], scalar=SCALE,
                                                      in1=dmat[:, :, c, :], op0=ALU.mult, op1=ALU.mult), sc_done)

                        def finish(c):
                            g = NT * q + c
                            dve.wait_ge(u_ready, g + 1)
                            dve.wait_ge(n_ready, g + 1)
                            for e in range(2):
                                r = slice(HD * e, HD * e + HD)
                                cs = Cst[r, e * (HD + 1):(e + 1) * (HD + 1)]
                                do(v.scalar_tensor_tensor(out=cs, in0=cs, scalar=cwb[r, c:c + 1],
                                                          in1=ps[r, 4 + c % 2, e * (HD + 1):(e + 1) * (HD + 1)],
                                                          op0=ALU.mult, op1=ALU.add), c_upd if e else None)
                            o = ps[:, 2 + c % 2, 0:2 * (HD + 1)].rearrange("p (e d) -> p e d", e=2)
                            do(v.scalar_tensor_tensor(out=den[:, :].unsqueeze(2), in0=o[:, :, HD:HD + 1], scalar=-1.0,
                                                      in1=em[:, c, 2 * q:2 * q + 2].unsqueeze(2), op0=ALU.mult, op1=ALU.max))
                            do(v.tensor_tensor(out=den[:, :].unsqueeze(2), in0=o[:, :, HD:HD + 1], in1=den[:, :].unsqueeze(2), op=ALU.max))
                            do(v.reciprocal(den[:, :], den[:, :]))
                            do(v.tensor_tensor(out=yb[:, c, :].rearrange("p (e d) -> p e d", e=2), in0=o[:, :, 0:HD],
                                               in1=den[:, :].unsqueeze(2).to_broadcast([P, 2, HD]), op=ALU.mult), n_read)

                        prepare(0)
                        for c in range(NT):
                            if c + 1 < NT:
                                prepare(c + 1)
                            finish(c)
                            if c == 2:
                                dve.wait_ge(o_exp, q + 1)
                                for zo, s in ((zt[:, 0:NT, OG:ZW], None), (zt[0:NB, NT, OG:ZW], og_done)):
                                    do(v.tensor_scalar(zo, zo, 1.0, None, ALU.add))
                                    do(v.reciprocal(zo, zo), s)
                        dve.wait_ge(ct_ready, q + 1)
                        do(v.tensor_copy(cT[:, 0:HD], ps[0:HD, 6, 0:HD]))
                        do(v.tensor_copy(cT[:, HD:P], ps[0:HD, 6, P + HD:2 * P]), ct_done)
                    sqv = att[:, 0:SEQ].rearrange("p (t c) -> p t c", t=NT)
                    ssum = ssq[:, 0:NT] if p < PAIRS else ssq[:, NT + 1:2 * NT + 1]
                    do(v.tensor_tensor(out=sqv, in0=yb[:, :, :], in1=yb[:, :, :], op=ALU.mult))
                    if h2 == 0:
                        do(v.tensor_reduce(out=ssum, in_=sqv, axis=AX.X, op=ALU.add), yb_done if p < PAIRS else None)
                    else:
                        do(v.tensor_reduce(out=yt2[:, 0:NT], in_=sqv, axis=AX.X, op=ALU.add))
                        do(v.tensor_tensor(out=ssum, in0=ssum, in1=yt2[:, 0:NT], op=ALU.add), yb_done if p < PAIRS else None)
                    if p >= PAIRS:
                        do(v.tensor_tensor(out=yb[:, :, :], in0=yb[:, :, :], in1=zt[:, 0:NT, OG:ZW], op=ALU.mult), yb_done)

                ztf = zt[:, :, :].rearrange("p t c -> p (t c)")
                dve.wait_ge(zb_in, 16 * 18)
                sall = att[:, 2560:2560 + 3 * HD].rearrange("p (r b h) -> p r b h", r=3, b=NB)
                for b in range(NB):
                    s = b % 3
                    dve.wait_ge(kv_in[s], 48 * (b // 3 + 1))
                    dve.wait_ge(q_in[b % 2], 16 * (b // 2 + 1))
                    kv = ztf[:, s * 1536:(s + 1) * 1536].rearrange("p (r c) -> p r c", r=3)
                    qd = (att[:, 1536:2048], att[:, 2048:2560])[b % 2]
                    pr = att[:, 0:1536].rearrange("p (r c) -> p r c", r=3)
                    do(v.tensor_tensor(out=pr, in0=kv, in1=qd.unsqueeze(1).to_broadcast([P, 3, WA]), op=ALU.mult), kq_used)
                    do(v.tensor_reduce(out=sall[:, :, b, :], in_=pr.rearrange("p r (h d) -> p r h d", h=NH), axis=AX.X, op=ALU.add),
                       s_scores if b == NB - 1 else None)
                sm = att[0:HD, 3072:3072 + 385]
                do(v.tensor_tensor(out=sv[:, 1, :], in0=zb[:, 0, :], in1=zb[:, 1, :], op=ALU.mult))
                do(v.tensor_reduce(out=small[:, 4:5], in_=sv[:, 1, :], axis=AX.X, op=ALU.add))
                do(v.tensor_scalar(sm[:, 384:385], small[:, 4:5], float(np.log(3.0) / SCALE), None, ALU.add))
                dve.wait_ge(st_ready, 1)
                do(v.tensor_copy(sm[:, 0:384], ps[0:HD, 0, 0:384]))
                do(v.tensor_reduce(out=small[:, 4:5], in_=sm, axis=AX.X, op=ALU.max))
                do(v.tensor_scalar(small[:, 10:11], small[:, 4:5], -SCALE, None, ALU.mult), sp_max)
                dve.wait_ge(sp_exp, 1)
                do(v.reciprocal(small[:, 12:13], small[:, 11:12]))
                do(v.tensor_scalar(sm, sm, small[:, 12:13], None, ALU.mult), pj_ready)
                dve.wait_ge(pj_back, 1)
                do(v.tensor_copy(att[:, 3584:3584 + 3 * HD], ps[:, 1, 0:3 * HD]), pj_done)
                do(v.tensor_scalar(sv[:, 2, :], zb[:, 2, :], sm[:, 384:385], None, ALU.mult))
                dve.wait_ge(v_used, NB)
                oT = att[:, 2048:2048 + 32].rearrange("p (c b) -> p c b", c=4)
                for c in range(4):
                    for e in range(2):
                        r = slice(HD * e, HD * e + HD)
                        src = ps[r, 2, c * 64:(c + 1) * 64].rearrange("p (b h) -> p b h", h=NH)[:, :, 2 * c + e]
                        do(v.tensor_copy(oT[r, c, :], src), ot_done if (c, e) == (3, 1) else None)
                dve.wait_ge(so_ready, 1)
                dve.wait_ge(yb_stored, 16 * 2 * PAIRS)
                do(v.tensor_copy(yb[0:NB, 0:4, :].rearrange("p t c -> p (t c)"), ps[0:NB, 3, :]), so_done)
                dve.wait_ge(as_in, 16)
                do(v.tensor_tensor(out=sv[:, 3, :], in0=sv[:, 3, :], in1=sv[:, 2, :], op=ALU.add))
                ig, lf, m0, m1 = (small[:, j:j + 1] for j in range(4))
                do(v.tensor_tensor(out=small[:, 5:6], in0=lf, in1=m0, op=ALU.add))
                do(v.tensor_tensor(out=m1, in0=small[:, 5:6], in1=ig, op=ALU.max))
                do(v.tensor_tensor(out=small[:, 7:8], in0=small[:, 5:6], in1=m1, op=ALU.subtract))
                do(v.tensor_tensor(out=small[:, 8:9], in0=ig, in1=m1, op=ALU.subtract))
                do(v.tensor_scalar(small[:, 9:10], m1, -1.0, None, ALU.mult), sc_exp_in)
                dve.wait_ge(sc_exp, 1)
                iw, ws, em1 = (small[:, j:j + 1] for j in (7, 8, 9))
                qb_, kb_, vb_ = zb[:, 3, :], zb[:, 4, :], zb[:, 5, :]
                do(v.tensor_scalar(kb_, kb_, SCALE, None, ALU.mult))
                do(v.tensor_tensor(out=sv[:, 1, :], in0=qb_, in1=kb_, op=ALU.mult))
                do(v.tensor_reduce(out=small[:, 12:13], in_=sv[:, 1, :], axis=AX.X, op=ALU.add))
                do(v.tensor_tensor(out=small[:, 12:13], in0=small[:, 12:13], in1=ws, op=ALU.mult))
                do(v.tensor_tensor(out=sv[:, 1, :], in0=qb_, in1=sv[:, 0, :], op=ALU.mult))
                do(v.tensor_reduce(out=small[:, 13:14], in_=sv[:, 1, :], axis=AX.X, op=ALU.add))
                do(v.scalar_tensor_tensor(out=small[:, 13:14], in0=small[:, 13:14], scalar=iw, in1=small[:, 12:13], op0=ALU.mult, op1=ALU.add))
                do(v.scalar_tensor_tensor(out=small[:, 14:15], in0=small[:, 13:14], scalar=-1.0, in1=em1, op0=ALU.mult, op1=ALU.max))
                do(v.tensor_tensor(out=small[:, 13:14], in0=small[:, 13:14], in1=small[:, 14:15], op=ALU.max))
                do(v.reciprocal(small[:, 13:14], small[:, 13:14]))
                dve.wait_ge(cst_in, 16)
                Cs = ztf[0:HD, 0:4096].rearrange("p (v k) -> p v k", v=HD)
                Ct = att[0:HD, 0:4096].rearrange("p (v k) -> p v k", v=HD)
                do(v.tensor_tensor(out=Ct, in0=Cs, in1=qb_.unsqueeze(1).to_broadcast([HD, HD, HD]), op=ALU.mult))
                do(v.tensor_reduce(out=sv[:, 1, :], in_=Ct, axis=AX.X, op=ALU.add))
                do(v.tensor_scalar(sv[:, 1, :], sv[:, 1, :], iw, None, ALU.mult))
                do(v.scalar_tensor_tensor(out=sv[:, 1, :], in0=vb_, scalar=small[:, 12:13], in1=sv[:, 1, :], op0=ALU.mult, op1=ALU.add))
                do(v.tensor_scalar(sv[:, 1, :], sv[:, 1, :], small[:, 13:14], None, ALU.mult))
                do(v.tensor_tensor(out=sv[:, 2, :], in0=sv[:, 1, :], in1=zb[:, 6, :], op=ALU.mult))
                do(v.tensor_scalar(kb_, kb_, ws, None, ALU.mult))
                do(v.scalar_tensor_tensor(out=sv[:, 0, :], in0=sv[:, 0, :], scalar=iw, in1=kb_, op0=ALU.mult, op1=ALU.add))
                do(v.tensor_tensor(out=Ct, in0=vb_.unsqueeze(2).to_broadcast([HD, HD, HD]), in1=kb_.unsqueeze(1).to_broadcast([HD, HD, HD]), op=ALU.mult))
                do(v.scalar_tensor_tensor(out=Cs, in0=Cs, scalar=iw, in1=Ct, op0=ALU.mult, op1=ALU.add), ys_done)
                dve.wait_ge(ys_in, 32)
                ysr = att[0:NB, 2048:3072]
                hs = yb[0:NB, 0:4, :].rearrange("p t c -> p (t c)")
                tmp = att[0:NB, 3072:3072 + WA]
                do(v.tensor_tensor(out=tmp, in0=ysr[:, 0:WA], in1=ysr[:, 0:WA], op=ALU.mult))
                do(v.tensor_reduce(out=ssq[0:NB, NT:NT + 1], in_=tmp, axis=AX.X, op=ALU.add))
                do(v.tensor_tensor(out=tmp, in0=hs, in1=hs, op=ALU.mult))
                do(v.tensor_reduce(out=ssq[0:NB, 2 * NT + 1:2 * NT + 2], in_=tmp, axis=AX.X, op=ALU.add), ssq_done)
                dve.wait_ge(yrs_first, 1)
                newton(do, yrs[:, :], yt2[:, :], [((lambda x: x), ssq[:, :])], WA, None)
                dve.wait_ge(ygain_in, 32)

                def normalise(t):
                    m = rows(t)
                    dve.wait_ge(yst_in[t % 2], 16 * (t // 2 + 1))
                    for h in range(2):
                        y = att[0:m, (t % 2) * D + h * WA:(t % 2) * D + (h + 1) * WA]
                        do(v.scalar_tensor_tensor(out=y, in0=y, scalar=yrs[0:m, h * (NT + 1) + t:h * (NT + 1) + t + 1],
                                                  in1=rowr[0:m, h * WA:(h + 1) * WA], op0=ALU.mult, op1=ALU.mult), yn_done if h else None)

                normalise(0)
                for t in range(NT + 1):
                    m = rows(t)
                    if t < NT:
                        normalise(t + 1)
                    for j in range(2):
                        dve.wait_ge(yh_done, 2 * t + j + 1)
                        z = ps[:, 2 * (t % 2) + j, 0:4 * m].rearrange("p (k m) -> p k m", k=4)
                        do(v.tensor_tensor(out=lo[:, 4 * j:4 * j + 4, tok(t)], in0=z, in1=hi[:, 4 * j:4 * j + 4, tok(t)].bitcast(F32),
                                           op=ALU.subtract), yl_done)
                dve.wait_ge(x_back, 16)
                for j in range(24):
                    b, c, o = j // 6, (j % 6) // 2, j % 2
                    dve.wait_ge(gemm_done, GEMM_OUT + j + 1)
                    x = X[:, 2 * b + o, col(c)]
                    do(v.tensor_tensor(out=x, in0=x, in1=ps[:, 4 + j % 4, 0:CH], op=ALU.add), wo_done, wait=(j == 23))
                dve_split(do, 1)
                dve_rstd(do, 1)
                do(v.memset(wa[:, 0:2], 0.0))

                def conv_tile(i, o):
                    gw = GEMM_FFN + 6 * o
                    for c in range(3):
                        dve.wait_ge(gemm_done, gw + c + 1 + 36 * i)
                        do(v.tensor_tensor(out=wa[:, 2 + c * CH:2 + (c + 1) * CH], in0=ps[:, c, 0:CH], in1=rstd[:, col(c)], op=ALU.mult),
                           gate_read, wait=(c == 2))
                    tl = tail[:, bass.ds(2 * i + o, 1), :].rearrange("p z n -> p (z n)")
                    cv = cvec[:, bass.ds(2 * i + o, 1), :].rearrange("p z n -> p (z n)")
                    do(v.tensor_copy(tl, wa[:, SEQ:SEQ + 2 + NB]), wait=False)
                    do(v.tensor_copy(cvt[:, :], cv))
                    tap = [cvt[:, 2 * NB + j:2 * NB + j + 1] for j in range(CW)]
                    bias = cvt[:, 2 * NB + CW:2 * NB + CW + 1]
                    st = cvt[:, 0:2 * NB].rearrange("p (b j) -> p b j", j=2)
                    do(v.tensor_scalar(wb[:, :], wa[:, 2:2 + TOK], tap[2], bias, ALU.mult, ALU.add))
                    for j in (1, 0):
                        do(v.scalar_tensor_tensor(out=wb[:, 0:SEQ], in0=wa[:, j:j + SEQ], scalar=tap[j], in1=wb[:, 0:SEQ],
                                                  op0=ALU.mult, op1=ALU.add), wait=False)
                        do(v.scalar_tensor_tensor(out=wb[:, SEQ:TOK], in0=st[:, :, j], scalar=tap[j], in1=wb[:, SEQ:TOK],
                                                  op0=ALU.mult, op1=ALU.add), conv_1 if j == 0 else None)
                    dve.wait_ge(gelu_done, 2 * i + o + 1)
                    do(v.tensor_tensor(out=wb[:, :], in0=wb[:, :], in1=rstd[:, :], op=ALU.mult))
                    for c in range(3):
                        dve.wait_ge(gemm_done, gw + 3 + c + 1 + 36 * i)
                        do(v.tensor_tensor(out=wb[:, col(c)], in0=wb[:, col(c)], in1=ps[:, 3 + (3 * o + c) % 2, 0:CH], op=ALU.mult), y_val)
                        dve.wait_ge(y_hi, 6 * i + 3 * o + c + 1)
                        do(v.tensor_tensor(out=ylo[:, o, col(c)], in0=wb[:, col(c)], in1=yhi[:, o, col(c)].bitcast(F32), op=ALU.subtract), y_lo)

                with dve.Fori(0, FG) as i:
                    do.loop(i, {dve_step: 2 * 7, gate_read: 6, conv_1: 2, y_val: 6, y_lo: 6, dn_read: 24})
                    for o in range(2):
                        conv_tile(i, o)
                    for j in range(24):
                        dve.wait_ge(gemm_done, GEMM_FFN + 12 + j + 1 + 36 * i)
                        x = X[:, j % 8, col(j // 8)]
                        do(v.tensor_tensor(out=x, in0=x, in1=ps[:, 5 + j % 3, 0:CH], op=ALU.add), dn_read, wait=(j == 23))
                    do.end_loop(FG)
                dve_split(do, 2)
                for t in range(NT + 1):
                    m = rows(t)
                    dve.wait_ge(pt_hi, t + 1)
                    z = ps[:, t % 2, 0:2 * m].rearrange("p (k m) -> p k m", k=2)
                    do(v.tensor_tensor(out=ylo[:, :, tok(t)], in0=z, in1=yhi[:, :, tok(t)].bitcast(F32), op=ALU.subtract), pt_lo)
                dve_rstd(do, 2)

                def scaled(j):
                    c = (j % 6) // 2
                    dve.wait_ge(gemm_done, GEMM_PLE + 2 * j + 1)
                    do(v.tensor_tensor(out=wa[:, col(j % 3)], in0=ps[:, j % 3, 0:CH], in1=rstd[:, col(c)], op=ALU.mult), pg_sc)

                scaled(0)
                for j in range(24):
                    b, c, o = j // 6, (j % 6) // 2, j % 2
                    if j + 1 < 24:
                        scaled(j + 1)
                    g = wa[:, col(j % 3)]
                    dve.wait_ge(pg_exp, j + 1)
                    do(v.tensor_scalar(g, g, 1.0, None, ALU.add))
                    do(v.reciprocal(g, g))
                    dve.wait_ge(gemm_done, GEMM_PLE + 2 * j + 2)
                    do(v.tensor_tensor(out=g, in0=g, in1=ps[:, 3 + j % 2, 0:CH], op=ALU.mult))
                    x = X[:, 2 * b + o, col(c)]
                    do(v.tensor_tensor(out=x, in0=x, in1=g, op=ALU.add), ple_done)
                for g in range(3):
                    w = min(8, FT - 8 * g) * P
                    dve.wait_ge(tl_ready, g + 1)
                    if g == 2:
                        dve.wait_ge(tl_stored, 64)
                    src = ps[0:2 + NB, 2 * g:2 * g + 2, :].rearrange("p b n -> p (b n)")[:, 0:w]
                    do(v.tensor_copy((wa, wb)[g % 2][0:2 + NB, 0:w], src), tl_done)
                end_layer(dve, l)
            for t in range(NT + 1):
                m = rows(t)
                dve.wait_ge(fin_turned, t + 1)
                if t >= 2:
                    dve.wait_ge(y_stored[t % 2], 16 * (t // 2))
                do0(v.tensor_copy((wa, wb)[t % 2][0:m, 512:D], ps[0:m, 2 * (t % 2) + 1, :]), fin_evac_v)


def constants():
    f = np.float32
    ident = np.eye(P, dtype=f)
    dist = np.arange(P)[:, None] + (NT - 1) * P - np.arange(SEQ)[None, :]
    count = sum(((dist >= 0) & (dist % d == 0) & (dist <= w)).astype(int) for w, d in DIL)
    mask = np.where(count > 0, np.log(np.maximum(count, 1)) / SCALE, NEG).astype(f)
    causal = np.where(np.arange(P)[None, :] >= np.arange(P)[:, None], 0.0, NEG).astype(f)
    inv = f(500000.0) ** (-np.arange(RH, dtype=f) / f(RH))
    pos = np.concatenate([np.arange(SEQ), np.full(P, PAST)]).astype(f)
    ang = (pos[:, None] * inv[None, :].astype(f)).astype(f).astype(np.float64)
    tab = np.concatenate([np.cos(ang), np.cos(ang), np.sin(ang), np.sin(ang)], axis=1).astype(f)
    rope = np.ascontiguousarray(tab.reshape(NT + 1, P, 4 * RH).transpose(1, 0, 2))
    sel = np.zeros((NH, NH, P), f)
    for h in range(NH):
        sel[h, h] = 1.0
    return {"c_ident": ident, "c_mask": mask, "c_causal": causal, "c_rope": rope, "c_sel": sel}


OUTS = [
    ("y_p", (1, SEQ, D)), ("y_s", (NB, 1, D)),
    ("wk_p", (DEPTH, 1, SEQ, NH, HD)), ("wv_p", (DEPTH, 1, SEQ, NH, HD)),
    ("C_p", (DEPTH, 1, NH, HD, HD)), ("n_p", (DEPTH, 1, NH, HD)), ("m_p", (DEPTH, 1, NH)),
    ("conv_p", (DEPTH, 1, CW - 1, DFF)),
    ("wk_s", (DEPTH, NB, 1, NH, HD)), ("wv_s", (DEPTH, NB, 1, NH, HD)),
    ("C_s", (DEPTH, NB, NH, HD, HD)), ("n_s", (DEPTH, NB, NH, HD)), ("m_s", (DEPTH, NB, NH)),
    ("conv_s", (DEPTH, NB, CW - 1, DFF)),
]


def kernel(**inputs):
    import numpy as _np
    import concourse.bacc as _bacc
    from concourse.bass_utils import run_bass_kernel_spmd as _run

    nc = _bacc.Bacc("TRN2", target_bir_lowering=False, num_devices=1, dynamic_dma_scratch_size=2048)
    arrays, A, O = {}, {}, {}
    for name, a in list(inputs.items()) + list(constants().items()):
        a = _np.ascontiguousarray(a)
        arrays[f"in_{name}"] = a
        A[name] = nc.dram_tensor(f"in_{name}", a.shape, mybir.dt.from_np(a.dtype), kind="ExternalInput").ap()
    for name, shape in OUTS:
        O[name] = nc.dram_tensor(f"out_{name}", shape, F32, kind="ExternalOutput").ap()
    build(nc, A, O)
    r = _run(nc, [arrays], core_ids=[0])
    return tuple(r.results[0][f"out_{name}"] for name, _ in OUTS)
```
